# Optimizing a Trainium2 kernel written in Bass

```python
import math
import jax
import jax.numpy as jnp
from jax import lax
import numpy as np

D_MODEL = 1024
BATCH = 1
SEQ = 1024
DEPTH = 1

GRID_W = 64
CTX_LEN = 256
N_MIXERS = 3
MIX_SHORTCONV = 0
MIX_HYENA = 1
MIX_ATTN = 2
CONV_W = 3
EPS = 1e-6
HY_ORDER = 2
HY_EMB = 33
HY_BANDS = (HY_EMB - 1) // 2
HY_FILTER_HIDDEN = 64
HY_FAST_DECAY = 0.3
HY_SLOW_DECAY = 1.5
HY_TARGET = 1e-2
HEAD_DIM = 128
N_Q_HEADS = D_MODEL // HEAD_DIM
N_KV_HEADS = 2
Q_PER_KV = N_Q_HEADS // N_KV_HEADS
AXIS_DIM = HEAD_DIM // 2
ROPE_THETA = 10000.0
Q_BLOCK = 128
N_EXPERTS = 16
EC_CAPACITY_FACTOR = 2
D_EXPERT = D_MODEL


def _layers_of(kind):
    return list(range(kind, DEPTH, N_MIXERS))

def rms_norm(x, g):
    xf = x.astype(jnp.float32)
    y = xf * lax.rsqrt(jnp.mean(xf * xf, axis=-1, keepdims=True) + EPS)
    return (y * g.astype(jnp.float32)).astype(x.dtype)

def modulate(x, shift, scale):
    return x * (1.0 + scale) + shift

def dwconv_centred(x, w):
    L = x.shape[1]
    p = CONV_W // 2
    xp = jnp.pad(x, ((0, 0), (p, p), (0, 0)))
    y = xp[:, 0:L] * w[0]
    for k in range(1, CONV_W):
        y = y + xp[:, k:k + L] * w[k]
    return y

def short_conv_mixer(h, w_in, conv_w, w_out):
    gate_b, gate_c, v = jnp.split(h @ w_in, 3, axis=-1)
    return (gate_b * dwconv_centred(gate_c * v, conv_w)) @ w_out

def hyena_filter_spectrum(L, w1, b1, w2, b2, w3, sin_freq):
    f32 = jnp.float32
    t = jnp.linspace(0.0, 1.0, L, dtype=f32)[:, None]
    bands = jnp.linspace(1e-4, HY_BANDS - 1, HY_BANDS, dtype=f32)[None, :]
    ang = (2.0 * math.pi / L) * jnp.arange(L, dtype=f32)[:, None] * bands
    z = jnp.concatenate([t, jnp.cos(ang), -jnp.sin(ang)], axis=-1)
    freq = sin_freq.astype(f32)
    a = jnp.sin(freq * (z @ w1.astype(f32) + b1.astype(f32)))
    a = jnp.sin(freq * (a @ w2.astype(f32) + b2.astype(f32)))
    h = (a @ w3.astype(f32)).reshape(L, 2, HY_ORDER, D_MODEL)
    deltas = jnp.abs(jnp.linspace(math.log(HY_TARGET) / HY_SLOW_DECAY,
                                  math.log(HY_TARGET) / HY_FAST_DECAY, D_MODEL, dtype=f32))
    h = h * jnp.exp(-t * deltas[None, :])[:, None, None, :]
    fwd = h[:, 0]
    bwd = h[1:, 1][::-1]
    full = jnp.concatenate([fwd, jnp.zeros((1, HY_ORDER, D_MODEL), f32), bwd], axis=0)
    full = full / jnp.sum(jnp.abs(full), axis=0, keepdims=True)
    return jnp.fft.rfft(full, axis=0)

def long_conv(u, filt_f, skip):
    L = u.shape[1]
    uf = u.astype(jnp.float32)
    y = jnp.fft.irfft(jnp.fft.rfft(uf, n=2 * L, axis=1) * filt_f[None], n=2 * L, axis=1)[:, :L]
    return (y + uf * skip.astype(jnp.float32)).astype(u.dtype)

def hyena_mixer(h, w_in, conv_w, f_w1, f_b1, f_w2, f_b2, f_w3, sin_freq, skip, w_out):
    L = h.shape[1]
    parts = jnp.split(dwconv_centred(h @ w_in, conv_w), HY_ORDER + 1, axis=-1)
    z, gates = parts[0], parts[1:]
    filt = hyena_filter_spectrum(L, f_w1, f_b1, f_w2, f_b2, f_w3, sin_freq)
    for o in range(HY_ORDER):
        z = gates[o] * long_conv(z, filt[:, o], skip[o])
    return z @ w_out

def axial_rope_tables(n_tokens, dtype):
    f32 = jnp.float32
    rows = n_tokens // GRID_W
    row = jnp.repeat(jnp.arange(rows, dtype=f32), GRID_W)
    col = jnp.tile(jnp.arange(GRID_W, dtype=f32), rows)
    inv = ROPE_THETA ** (-jnp.arange(0, AXIS_DIM, 2, dtype=f32) / AXIS_DIM)

    def axis_angles(pos):
        a = pos[:, None] * inv[None, :]
        return jnp.concatenate([a, a], axis=-1)

    ang = jnp.concatenate([axis_angles(row), axis_angles(col)], axis=-1)
    return jnp.cos(ang).astype(dtype), jnp.sin(ang).astype(dtype)

def _rotate_axial(x):
    q = AXIS_DIM // 2
    xr, xc = x[..., :AXIS_DIM], x[..., AXIS_DIM:]
    return jnp.concatenate([-xr[..., q:], xr[..., :q], -xc[..., q:], xc[..., :q]], axis=-1)

def apply_rope(x, cos, sin):
    return x * cos + _rotate_axial(x) * sin

def _attend(q, k, v):
    s = jnp.einsum('bqkgd,bskd->bkgqs', q, k, preferred_element_type=jnp.float32) * (HEAD_DIM ** -0.5)
    p = jax.nn.softmax(s, axis=-1)
    return jnp.einsum('bkgqs,bskd->bqkgd', p.astype(v.dtype), v)

def gqa_mixer(h_lat, h_ctx, w_qkv, q_g, k_g, w_o, ctx_out):
    B, L, _ = h_lat.shape
    Lc = h_ctx.shape[1]
    QD = N_Q_HEADS * HEAD_DIM
    KVD = N_KV_HEADS * HEAD_DIM

    def heads_q(t, n):
        return rms_norm(t.reshape(B, n, N_KV_HEADS, Q_PER_KV, HEAD_DIM), q_g)

    def heads_kv(t, n):
        k = rms_norm(t[..., :KVD].reshape(B, n, N_KV_HEADS, HEAD_DIM), k_g)
        v = t[..., KVD:].reshape(B, n, N_KV_HEADS, HEAD_DIM)
        return k, v

    qkv_l = h_lat @ w_qkv
    q_l = heads_q(qkv_l[..., :QD], L)
    k_l, v_l = heads_kv(qkv_l[..., QD:], L)
    cos, sin = axial_rope_tables(L, q_l.dtype)
    q_l = apply_rope(q_l, cos[None, :, None, None], sin[None, :, None, None])
    k_l = apply_rope(k_l, cos[None, :, None], sin[None, :, None])
    if ctx_out:
        qkv_c = h_ctx @ w_qkv
        q_c = heads_q(qkv_c[..., :QD], Lc)
        kv_c = qkv_c[..., QD:]
    else:
        kv_c = h_ctx @ w_qkv[:, QD:]
    k_c, v_c = heads_kv(kv_c, Lc)

    k_all = jnp.concatenate([k_c, k_l], axis=1)
    v_all = jnp.concatenate([v_c, v_l], axis=1)
    n_blk = L // Q_BLOCK
    qb = jnp.moveaxis(q_l.reshape(B, n_blk, Q_BLOCK, N_KV_HEADS, Q_PER_KV, HEAD_DIM), 1, 0)
    o_l = lax.map(lambda qblk: _attend(qblk, k_all, v_all), qb)
    y_l = jnp.moveaxis(o_l, 0, 1).reshape(B, L, QD) @ w_o
    y_c = _attend(q_c, k_c, v_c).reshape(B, Lc, QD) @ w_o if ctx_out else None
    return y_l, y_c

def expert_choice_ffn(h, w_router, w_gate, w_up, w_down):
    B, N, D = h.shape
    cap = EC_CAPACITY_FACTOR * N // N_EXPERTS
    aff = jax.nn.softmax((h @ w_router).astype(jnp.float32), axis=-1)
    g, idx = lax.top_k(jnp.swapaxes(aff, 1, 2), cap)
    xs = jax.vmap(lambda hb, ib: hb[ib])(h, idx)
    hid = jax.nn.silu(jnp.einsum('becd,edf->becf', xs, w_gate)) * jnp.einsum('becd,edf->becf', xs, w_up)
    ys = jnp.einsum('becf,efd->becd', hid, w_down) * g[..., None].astype(h.dtype)
    return jax.vmap(lambda yb, ib: jnp.zeros((N, D), yb.dtype).at[ib.reshape(-1)].add(yb.reshape(-1, D)))(ys, idx)

def first_inputs(seed: int = 0) -> dict:
    key = jax.random.key(seed)
    ks = iter(jax.random.split(key, 40))
    D, F = D_MODEL, D_EXPERT
    nA, nB, nC = (len(_layers_of(k)) for k in range(N_MIXERS))
    QKV = (N_Q_HEADS + 2 * N_KV_HEADS) * HEAD_DIM

    def nrm(shape, s):
        return jax.random.normal(next(ks), shape, jnp.float32) * s

    return {
        "x": nrm((BATCH, SEQ, D), 1.0),
        "c": nrm((BATCH, D), 1.0),
        "ctx": nrm((BATCH, CTX_LEN, D), 1.0),
        "c_ctx": nrm((D,), 1.0),
        "ada_w": nrm((DEPTH, D, 6 * D), 0.5 * D ** -0.5),
        "ada_b": nrm((DEPTH, 6 * D), 0.01),
        "norm_g": 1.0 + nrm((DEPTH, 2, D), 0.02),
        "sc_w_in": nrm((nA, D, 3 * D), D ** -0.5),
        "sc_conv": nrm((nA, CONV_W, D), CONV_W ** -0.5),
        "sc_w_out": nrm((nA, D, D), D ** -0.5),
        "hy_w_in": nrm((nB, D, (HY_ORDER + 1) * D), D ** -0.5),
        "hy_conv": nrm((nB, CONV_W, (HY_ORDER + 1) * D), CONV_W ** -0.5),
        "hy_f_w1": nrm((nB, HY_EMB, HY_FILTER_HIDDEN), HY_EMB ** -0.5),
        "hy_f_b1": nrm((nB, HY_FILTER_HIDDEN), 0.02),
        "hy_f_w2": nrm((nB, HY_FILTER_HIDDEN, HY_FILTER_HIDDEN), HY_FILTER_HIDDEN ** -0.5),
        "hy_f_b2": nrm((nB, HY_FILTER_HIDDEN), 0.02),
        "hy_f_w3": nrm((nB, HY_FILTER_HIDDEN, 2 * HY_ORDER * D), HY_FILTER_HIDDEN ** -0.5),
        "hy_sin_freq": 1.0 + nrm((nB, HY_FILTER_HIDDEN), 0.02),
        "hy_skip": nrm((nB, HY_ORDER, D), 1.0),
        "hy_w_out": nrm((nB, D, D), D ** -0.5),
        "at_w_qkv": nrm((nC, D, QKV), D ** -0.5),
        "at_q_g": 1.0 + nrm((nC, HEAD_DIM), 0.02),
        "at_k_g": 1.0 + nrm((nC, HEAD_DIM), 0.02),
        "at_w_o": nrm((nC, N_Q_HEADS * HEAD_DIM, D), (N_Q_HEADS * HEAD_DIM) ** -0.5),
        "moe_router": nrm((DEPTH, D, N_EXPERTS), D ** -0.5),
        "moe_w_gate": nrm((DEPTH, N_EXPERTS, D, F), D ** -0.5),
        "moe_w_up": nrm((DEPTH, N_EXPERTS, D, F), D ** -0.5),
        "moe_w_down": nrm((DEPTH, N_EXPERTS, F, D), F ** -0.5),
    }

def first_block(x, c, ctx, c_ctx, ada_w, ada_b, norm_g, sc_w_in, sc_conv, sc_w_out,
              hy_w_in, hy_conv, hy_f_w1, hy_f_b1, hy_f_w2, hy_f_b2, hy_f_w3, hy_sin_freq, hy_skip, hy_w_out,
              at_w_qkv, at_q_g, at_k_g, at_w_o, moe_router, moe_w_gate, moe_w_up, moe_w_down):
    last_attn = max(_layers_of(MIX_ATTN), default=-1)
    lat, cx = x, ctx
    silu_c = jax.nn.silu(c)
    silu_cc = jax.nn.silu(c_ctx)
    for i in range(DEPTH):
        kind = i % N_MIXERS
        j = i // N_MIXERS
        need_ctx = i <= last_attn
        upd_ctx = i < last_attn

        m_l = (silu_c @ ada_w[i] + ada_b[i])[:, None, :]
        sh1, sc1, g1, sh2, sc2, g2 = jnp.split(m_l, 6, axis=-1)
        hl = modulate(rms_norm(lat, norm_g[i, 0]), sh1, sc1)
        if need_ctx:
            m_c = silu_cc @ ada_w[i] + ada_b[i]
            csh1, csc1, cg1, csh2, csc2, cg2 = jnp.split(m_c, 6, axis=-1)
            hc = modulate(rms_norm(cx, norm_g[i, 0]), csh1, csc1)

        yc = None
        if kind == MIX_SHORTCONV:
            yl = short_conv_mixer(hl, sc_w_in[j], sc_conv[j], sc_w_out[j])
            if upd_ctx:
                yc = short_conv_mixer(hc, sc_w_in[j], sc_conv[j], sc_w_out[j])
        elif kind == MIX_HYENA:
            hy_args = (hy_w_in[j], hy_conv[j], hy_f_w1[j], hy_f_b1[j], hy_f_w2[j], hy_f_b2[j],
                       hy_f_w3[j], hy_sin_freq[j], hy_skip[j], hy_w_out[j])
            yl = hyena_mixer(hl, *hy_args)
            if upd_ctx:
                yc = hyena_mixer(hc, *hy_args)
        else:
            yl, yc = gqa_mixer(hl, hc, at_w_qkv[j], at_q_g[j], at_k_g[j], at_w_o[j], upd_ctx)

        lat = lat + g1 * yl
        hl2 = modulate(rms_norm(lat, norm_g[i, 1]), sh2, sc2)
        lat = lat + g2 * expert_choice_ffn(hl2, moe_router[i], moe_w_gate[i], moe_w_up[i], moe_w_down[i])
        if upd_ctx:
            cx = cx + cg1 * yc
            hc2 = modulate(rms_norm(cx, norm_g[i, 1]), csh2, csc2)
            cx = cx + cg2 * expert_choice_ffn(hc2, moe_router[i], moe_w_gate[i], moe_w_up[i], moe_w_down[i])
    return lat


CHUNK = 64
D_MLSTM = D_MODEL // 2
D_POOL = D_MODEL - D_MLSTM
N_HEADS = 4
HEAD_DIM_2 = D_MLSTM // N_HEADS
CONV_WIDTH = 4
POOL_WINDOWS = (2, 4, 8, 16)
N_POOL_GROUPS = len(POOL_WINDOWS)
POOL_GROUP_DIM = D_POOL // N_POOL_GROUPS
N_EXPERT_GROUPS = 4
EXPERTS_PER_GROUP = 8
N_EXPERTS_2 = N_EXPERT_GROUPS * EXPERTS_PER_GROUP
TOP_K = 2
D_EXPERT_2 = D_MODEL // 2
MOE_BLOCK = 128

COL_U = 0
COL_V = COL_U + D_MLSTM
COL_O = COL_V + D_MLSTM
COL_I = COL_O + D_MLSTM
COL_F = COL_I + N_HEADS
COL_P = COL_F + N_HEADS
IN_COLS = COL_P + D_POOL


def rms_norm_2(x, g):
    xf = x.astype(jnp.float32)
    y = xf * lax.rsqrt(jnp.mean(xf * xf, axis=-1, keepdims=True) + EPS)
    return (y * g.astype(jnp.float32)).astype(x.dtype)

def causal_conv(x, w, b):
    k_w, ch = w.shape
    y = lax.conv_general_dilated(x, w[:, None, :], window_strides=(1,), padding=[(k_w - 1, 0)],
                                 dimension_numbers=('NWC', 'WIO', 'NWC'), feature_group_count=ch)
    return y + b

def mlstm_chunkwise(q, k, v, i_pre, f_pre):
    bsz, nh, seq, dh = q.shape
    nc = seq // CHUNK
    q = q.astype(jnp.float32) * (dh ** -0.5)
    k = k.astype(jnp.float32)
    v = v.astype(jnp.float32)
    log_i = i_pre.astype(jnp.float32)
    log_f = jax.nn.log_sigmoid(f_pre.astype(jnp.float32))

    def to_chunks(a):
        return jnp.moveaxis(a.reshape(bsz, nh, nc, CHUNK, *a.shape[3:]), 2, 0)

    qc, kc, vc, ic = to_chunks(q), to_chunks(k), to_chunks(v), to_chunks(log_i)
    bc = jnp.cumsum(to_chunks(log_f), axis=-1)
    causal = jnp.tril(jnp.ones((CHUNK, CHUNK), dtype=bool))

    def step(carry, inp):
        c_st, n_st, m_st = carry
        q_, k_, v_, ig, b_ = inp
        d_log = b_[..., :, None] - b_[..., None, :] + ig[..., None, :]
        d_log = jnp.where(causal, d_log, -jnp.inf)
        inter = b_ + m_st[..., None]
        m_t = jnp.maximum(inter, jnp.max(d_log, axis=-1))
        w_intra = jnp.exp(d_log - m_t[..., None])
        a_inter = jnp.exp(inter - m_t)
        s = jnp.einsum('bhtd,bhsd->bhts', q_, k_) * w_intra
        num = (a_inter[..., None] * jnp.einsum('bhed,bhtd->bhte', c_st, q_)
               + jnp.einsum('bhts,bhse->bhte', s, v_))
        den = a_inter * jnp.einsum('bhd,bhtd->bht', n_st, q_) + jnp.sum(s, axis=-1)
        h = num / jnp.maximum(jnp.abs(den), jnp.exp(-m_t))[..., None]
        b_last = b_[..., -1]
        w_log = b_last[..., None] - b_ + ig
        m_new = jnp.maximum(b_last + m_st, jnp.max(w_log, axis=-1))
        a_prev = jnp.exp(b_last + m_st - m_new)
        w_s = jnp.exp(w_log - m_new[..., None])
        c_new = a_prev[..., None, None] * c_st + jnp.einsum('bhs,bhse,bhsd->bhed', w_s, v_, k_)
        n_new = a_prev[..., None] * n_st + jnp.einsum('bhs,bhsd->bhd', w_s, k_)
        return (c_new, n_new, m_new), h

    init = (jnp.zeros((bsz, nh, dh, dh), jnp.float32), jnp.zeros((bsz, nh, dh), jnp.float32),
            jnp.zeros((bsz, nh), jnp.float32))
    _, hs = lax.scan(step, init, (qc, kc, vc, ic, bc))
    return jnp.moveaxis(hs, 0, 2).reshape(bsz, nh, seq, dh)

def mlstm_group(u, v, o_pre, i_pre, f_pre, conv_w, conv_b, w_q, w_k, b_i, b_f, norm_g, skip):
    bsz, seq, _ = u.shape
    uc = jax.nn.silu(causal_conv(u, conv_w, conv_b))
    uh = uc.reshape(bsz, seq, N_HEADS, HEAD_DIM_2)
    q = jnp.einsum('bshd,hde->bhse', uh, w_q)
    k = jnp.einsum('bshd,hde->bhse', uh, w_k)
    vh = v.reshape(bsz, seq, N_HEADS, HEAD_DIM_2).transpose(0, 2, 1, 3)
    ig = (i_pre + b_i).transpose(0, 2, 1)
    fg = (f_pre + b_f).transpose(0, 2, 1)
    h = mlstm_chunkwise(q, k, vh, ig, fg)
    h = h * lax.rsqrt(jnp.mean(h * h, axis=-1, keepdims=True) + EPS)
    h = h * norm_g.astype(jnp.float32).reshape(N_HEADS, 1, HEAD_DIM_2)
    h = h.transpose(0, 2, 1, 3).reshape(bsz, seq, D_MLSTM)
    out = jax.nn.sigmoid(o_pre.astype(jnp.float32)) * (h + skip.astype(jnp.float32) * uc.astype(jnp.float32))
    return out.astype(u.dtype)

def pool_group(p, w_pool, b_pool, pool_scale):
    bsz, seq, _ = p.shape
    pf = p.astype(jnp.float32).reshape(bsz, seq, N_POOL_GROUPS, POOL_GROUP_DIM)
    cs = jnp.pad(jnp.cumsum(pf, axis=1), ((0, 0), (1, 0), (0, 0), (0, 0)))
    t = jnp.arange(seq, dtype=jnp.int32)
    win = jnp.array(POOL_WINDOWS, dtype=jnp.int32)
    start = jnp.maximum(t[:, None] + 1 - win[None, :], 0)
    lo = cs[:, start, jnp.arange(N_POOL_GROUPS)[None, :]]
    count = jnp.minimum(t[:, None] + 1, win[None, :]).astype(jnp.float32)
    pooled = (cs[:, 1:] - lo) / count[None, :, :, None] - pf
    y = jnp.einsum('bsgc,gcd->bsgd', pooled, w_pool.astype(jnp.float32)).reshape(bsz, seq, D_POOL)
    y = (y + b_pool.astype(jnp.float32)) * pool_scale.astype(jnp.float32)
    return y.astype(p.dtype)

def hierarchical_moe(h, w_rg, b_rg, w_re, b_re, w_gate, w_up, w_down):
    bsz, seq, dm = h.shape
    n_tok = bsz * seq
    hf = h.reshape(n_tok, dm)
    g_logits = (hf @ w_rg + b_rg).astype(jnp.float32)
    g_prob = jax.nn.softmax(g_logits, axis=-1)
    g_idx = jnp.argmax(g_logits, axis=-1).astype(jnp.int32)
    g_gate = jnp.take_along_axis(g_prob, g_idx[:, None], axis=1)[:, 0]
    e_logits = (hf @ w_re + b_re).astype(jnp.float32).reshape(n_tok, N_EXPERT_GROUPS, EXPERTS_PER_GROUP)
    e_logits = jnp.take_along_axis(e_logits, g_idx[:, None, None], axis=1)[:, 0]
    top_val, top_loc = lax.top_k(e_logits, TOP_K)
    gates = jax.nn.softmax(top_val, axis=-1) * g_gate[:, None]
    expert = g_idx[:, None] * EXPERTS_PER_GROUP + top_loc.astype(jnp.int32)
    n_asg = n_tok * TOP_K
    flat_e = expert.reshape(n_asg)
    flat_tok = jnp.repeat(jnp.arange(n_tok, dtype=jnp.int32), TOP_K)
    flat_gate = gates.reshape(n_asg)
    order = jnp.argsort(flat_e)
    sorted_e = flat_e[order]
    counts = jnp.bincount(flat_e, length=N_EXPERTS_2).astype(jnp.int32)
    starts = jnp.cumsum(counts) - counts
    padded = (counts + MOE_BLOCK - 1) // MOE_BLOCK * MOE_BLOCK
    pad_ends = jnp.cumsum(padded)
    pad_starts = pad_ends - padded
    rank = jnp.arange(n_asg, dtype=jnp.int32) - starts[sorted_e]
    dest = pad_starts[sorted_e] + rank
    n_blocks = (n_asg + MOE_BLOCK - 1) // MOE_BLOCK + N_EXPERTS_2
    n_slots = n_blocks * MOE_BLOCK
    slot_tok = jnp.full((n_slots,), n_tok, jnp.int32).at[dest].set(flat_tok[order])
    slot_gate = jnp.zeros((n_slots,), jnp.float32).at[dest].set(flat_gate[order])
    block_pos = jnp.arange(n_blocks, dtype=jnp.int32) * MOE_BLOCK
    block_expert = jnp.minimum(jnp.searchsorted(pad_ends, block_pos, side='right'), N_EXPERTS_2 - 1)

    def run_block(args):
        tok, e = args
        xb = hf[jnp.minimum(tok, n_tok - 1)]
        a = xb @ w_gate[e]
        b = xb @ w_up[e]
        return (jax.nn.silu(a) * b) @ w_down[e]

    out = lax.map(run_block, (slot_tok.reshape(n_blocks, MOE_BLOCK), block_expert))
    out = (out.reshape(n_slots, dm).astype(jnp.float32) * slot_gate[:, None]).astype(h.dtype)
    y = jnp.zeros((n_tok, dm), h.dtype).at[slot_tok].add(out, mode='drop')
    return y.reshape(bsz, seq, dm)

def second_inputs(seed: int = 0) -> dict:
    key = jax.random.key(seed)
    ks = jax.random.split(key, 28)
    L = DEPTH

    def nrm(k, shape, scale):
        return jax.random.normal(k, shape, jnp.float32) * scale

    return {
        'x': nrm(ks[0], (BATCH, SEQ, D_MODEL), 1.0),
        'c': nrm(ks[1], (BATCH, D_MODEL), 1.0),
        'ada_w': nrm(ks[2], (L, D_MODEL, 6 * D_MODEL), D_MODEL ** -0.5),
        'ada_b': nrm(ks[3], (L, 6 * D_MODEL), 0.02),
        'norm1_g': 1.0 + nrm(ks[4], (L, D_MODEL), 0.02),
        'w_in': nrm(ks[5], (L, D_MODEL, IN_COLS), D_MODEL ** -0.5),
        'conv_w': nrm(ks[6], (L, CONV_WIDTH, D_MLSTM), CONV_WIDTH ** -0.5),
        'conv_b': nrm(ks[7], (L, D_MLSTM), 0.02),
        'w_q': nrm(ks[8], (L, N_HEADS, HEAD_DIM_2, HEAD_DIM_2), HEAD_DIM_2 ** -0.5),
        'w_k': nrm(ks[9], (L, N_HEADS, HEAD_DIM_2, HEAD_DIM_2), HEAD_DIM_2 ** -0.5),
        'b_igate': nrm(ks[10], (L, N_HEADS), 0.1),
        'b_fgate': jnp.linspace(3.0, 6.0, N_HEADS, dtype=jnp.float32)[None, :] + nrm(ks[11], (L, N_HEADS), 0.1),
        'mlstm_norm_g': 1.0 + nrm(ks[12], (L, D_MLSTM), 0.02),
        'mlstm_skip': 1.0 + nrm(ks[13], (L, D_MLSTM), 0.1),
        'w_pool': nrm(ks[14], (L, N_POOL_GROUPS, POOL_GROUP_DIM, POOL_GROUP_DIM), POOL_GROUP_DIM ** -0.5),
        'b_pool': nrm(ks[15], (L, D_POOL), 0.02),
        'pool_scale': 1.0 + nrm(ks[16], (L, D_POOL), 0.1),
        'w_out': nrm(ks[17], (L, D_MODEL, D_MODEL), D_MODEL ** -0.5),
        'norm2_g': 1.0 + nrm(ks[18], (L, D_MODEL), 0.02),
        'w_router_group': nrm(ks[19], (L, D_MODEL, N_EXPERT_GROUPS), D_MODEL ** -0.5),
        'b_router_group': nrm(ks[20], (L, N_EXPERT_GROUPS), 0.01),
        'w_router_expert': nrm(ks[21], (L, D_MODEL, N_EXPERTS_2), D_MODEL ** -0.5),
        'b_router_expert': nrm(ks[22], (L, N_EXPERTS_2), 0.01),
        'w_expert_gate': nrm(ks[23], (L, N_EXPERTS_2, D_MODEL, D_EXPERT_2), D_MODEL ** -0.5),
        'w_expert_up': nrm(ks[24], (L, N_EXPERTS_2, D_MODEL, D_EXPERT_2), D_MODEL ** -0.5),
        'w_expert_down': nrm(ks[25], (L, N_EXPERTS_2, D_EXPERT_2, D_MODEL), D_EXPERT_2 ** -0.5),
        'final_g': 1.0 + nrm(ks[26], (D_MODEL,), 0.02),
    }

def second_block(x, c, ada_w, ada_b, norm1_g, w_in, conv_w, conv_b, w_q, w_k, b_igate, b_fgate,
              mlstm_norm_g, mlstm_skip, w_pool, b_pool, pool_scale, w_out, norm2_g,
              w_router_group, b_router_group, w_router_expert, b_router_expert,
              w_expert_gate, w_expert_up, w_expert_down, final_g):
    bsz, seq, dm = x.shape
    for l in range(DEPTH):
        mod = (jax.nn.silu(c) @ ada_w[l] + ada_b[l]).reshape(bsz, 6, dm)
        shift_a, scale_a, gate_a = mod[:, 0, None, :], mod[:, 1, None, :], mod[:, 2, None, :]
        shift_f, scale_f, gate_f = mod[:, 3, None, :], mod[:, 4, None, :], mod[:, 5, None, :]
        h = rms_norm_2(x, norm1_g[l]) * (1.0 + scale_a) + shift_a
        proj = h @ w_in[l]
        y_m = mlstm_group(proj[..., COL_U:COL_V], proj[..., COL_V:COL_O], proj[..., COL_O:COL_I],
                          proj[..., COL_I:COL_F], proj[..., COL_F:COL_P], conv_w[l], conv_b[l],
                          w_q[l], w_k[l], b_igate[l], b_fgate[l], mlstm_norm_g[l], mlstm_skip[l])
        y_p = pool_group(proj[..., COL_P:IN_COLS], w_pool[l], b_pool[l], pool_scale[l])
        mix = jnp.concatenate([y_m, y_p], axis=-1) @ w_out[l]
        x = x + gate_a * mix
        h = rms_norm_2(x, norm2_g[l]) * (1.0 + scale_f) + shift_f
        x = x + gate_f * hierarchical_moe(h, w_router_group[l], b_router_group[l], w_router_expert[l],
                                          b_router_expert[l], w_expert_gate[l], w_expert_up[l],
                                          w_expert_down[l])
    return rms_norm_2(x, final_g)


def setup_inputs(seed=0):
    out = dict(first_inputs(seed))
    for name, value in second_inputs(seed + 1).items():
        if name != "x":
            out[name + "_2"] = value
    return out


def reference(
    x, c, ctx, c_ctx, ada_w, ada_b, norm_g, sc_w_in, sc_conv, sc_w_out, hy_w_in, hy_conv,
    hy_f_w1, hy_f_b1, hy_f_w2, hy_f_b2, hy_f_w3, hy_sin_freq, hy_skip, hy_w_out, at_w_qkv,
    at_q_g, at_k_g, at_w_o, moe_router, moe_w_gate, moe_w_up, moe_w_down, c_2, ada_w_2, ada_b_2,
    norm1_g_2, w_in_2, conv_w_2, conv_b_2, w_q_2, w_k_2, b_igate_2, b_fgate_2, mlstm_norm_g_2,
    mlstm_skip_2, w_pool_2, b_pool_2, pool_scale_2, w_out_2, norm2_g_2, w_router_group_2,
    b_router_group_2, w_router_expert_2, b_router_expert_2, w_expert_gate_2, w_expert_up_2,
    w_expert_down_2, final_g_2,
):
    x = first_block(
        x, c, ctx, c_ctx, ada_w, ada_b, norm_g, sc_w_in, sc_conv, sc_w_out, hy_w_in, hy_conv,
        hy_f_w1, hy_f_b1, hy_f_w2, hy_f_b2, hy_f_w3, hy_sin_freq, hy_skip, hy_w_out, at_w_qkv,
        at_q_g, at_k_g, at_w_o, moe_router, moe_w_gate, moe_w_up, moe_w_down,
    )
    return second_block(
        x, c_2, ada_w_2, ada_b_2, norm1_g_2, w_in_2, conv_w_2, conv_b_2, w_q_2, w_k_2,
        b_igate_2, b_fgate_2, mlstm_norm_g_2, mlstm_skip_2, w_pool_2, b_pool_2, pool_scale_2,
        w_out_2, norm2_g_2, w_router_group_2, b_router_group_2, w_router_expert_2,
        b_router_expert_2, w_expert_gate_2, w_expert_up_2, w_expert_down_2, final_g_2,
    )


_drawn_inputs = setup_inputs


def setup_inputs(seed=0):
    import zlib

    import numpy as np

    out = dict(_drawn_inputs(seed))
    spreads = {}
    factors = {'conv_b_2': 2.721,
     'b_igate_2': 64.0,
     'mlstm_norm_g_2': 4.834,
     'b_pool_2': 2.708,
     'b_router_group_2': 12.265,
     'b_router_expert_2': 4.507,
     'final_g_2': 7.713}
    for name, (base, spread) in spreads.items():
        noise = np.random.default_rng([zlib.crc32(name.encode()), seed]).standard_normal(out[name].shape)
        drawn = base * np.exp(spread * noise) if base else spread * noise
        out[name] = jnp.asarray(drawn.astype(out[name].dtype))
    for name, factor in factors.items():
        out[name] = (out[name] * factor).astype(out[name].dtype)
    return out
```

```python
from contextlib import ExitStack

import concourse.bass as bass
from concourse import mybir
from concourse.alu_op_type import AluOpType as ALU

F32 = mybir.dt.float32
F32R = mybir.dt.float32r
U32 = mybir.dt.uint32
ACT = mybir.ActivationFunctionType
AX = mybir.AxisListType.X

P = 128
D = 1024
T = 1024
NT = T // P
KD = D // P
EPS = 1e-6
RING = 12
SPLIT_RING = 6
ADA_RING = 4
WSETS = 6
E1 = 16
CAP1 = 2 * T // E1
E2 = 32
F2 = 512
NR2 = 4 + E2

SEMS = """
    h2_done x1_done var2 rstd2 h2_out diag_used bc_done y_ready zs_hi tr2 h2T_ready sq2 diag_ready zs_lo
    rt_done wait_passed ada_done split_done z_done m1_lo hy_done pool_out unused_zero m2_y final_done consts
    masks var_ready rstd_ready stored m1_tok m1_y_done zero_row tok_zero ov_over rows_zero rows_in small_in
    silu_ready sq_done mod_ready tr_ready tr_hi split_hi f_part cv_done c_copied route1 e1_exp m1_used m1_hi
    m1_xT m1_xT_hi slots_ready m1_silu m1_hT m1_hT_hi if_hi v_even gate_exp branch d2_out uc_ready cell_in
    q_mm m_mm dmask pm_ready m_out wt_diag wt_rest pv hn_tr num_out final_in dve_steps cols_tr mod_mm xn_done
    tr_lo aff_ready affT_tr m1_xT_lo m1_hid m1_hT_lo if_lo v_odd if_mm gt_ready pool_mm k_mm k_out s_mm
    hn_ready q_out
"""


class Steps:

    def __init__(self, eng, sem):
        self.eng, self.sem, self.n, self.extra = eng, sem, 0, 0

    def mark(self, ins):
        ins.then_inc(self.sem, 1)
        self.n += 1

    def wait(self):
        self.eng.wait_ge(self.sem, self.extra + self.n)


def in_pairs(eng, count, body, steps=None, per=0):
    turns = (count - 2) // 2
    body(0, 0)
    at = steps.n if steps else 0
    body(0, 1)
    body(1, 0)
    if steps:
        assert steps.n == at + per, (steps.n, at, per)
    with eng.Fori(1, turns) as i:
        if steps:
            steps.extra = (i - 1) * per
        body(i, 1)
        body(i + 1, 0)
    if steps:
        assert steps.n == at + 2 * per, (steps.n, at, per)
        steps.extra, steps.n = 0, at + per * turns
    for s in range(2 * turns + 1, count):
        body(s // 2, s % 2)


def program(nc, io, out, room=P):
    with ExitStack() as ctx:
        build(nc, ctx, io, out, room)


def build(nc, ctx, io, out, room):
    def sb(name, shape, dt=F32, scope=ctx):
        return scope.enter_context(nc.sbuf_tensor(name, shape, dt))

    def dram(name, shape, dt=F32):
        return nc.dram_tensor(name, shape, dt).ap()

    NOVF = (2 * T - 1) // P if room == P else 2 * T // (room + 1)
    NBLK = E2 + NOVF

    x1_dram = dram("x1_dram", [T, D])
    h2_dram = dram("h2_dram", [T, D])
    x3_dram = dram("x3_dram", [T, D])
    h4_dram = dram("h4_dram", [T, D])
    tok_dram = dram("tok_dram", [NBLK * P, 1], U32)
    yslot_dram = dram("yslot_dram", [NBLK * P, D])

    ring = sb("ring", [P, RING, D])
    rows = sb("rows", [P, 2, P])
    cols = sb("cols", [P, 2, P])
    silu_c = sb("silu_c", [P, 16])
    mod = sb("mod", [P, 2, 48])
    gain = sb("gain", [P, 4, 8])
    ident = sb("ident", [P, P])
    ones = sb("ones", [P, P])
    diag = sb("diag", [P, 2, P])
    neghalf = sb("neghalf", [P, 8])
    stat = sb("stat", [P, 12, 8])
    router1 = sb("router1", [P, KD, E1])
    router2 = sb("router2", [P, KD, NR2])
    bias2 = sb("bias2", [P, NR2])
    gbias = sb("gbias", [4, 2])
    w_if = sb("w_if", [P, KD, 8])
    w_ifH = sb("w_ifH", [P, KD, 8], F32R)
    w_ifL = sb("w_ifL", [P, KD, 8], F32R)
    iota8 = sb("iota8", [P, 8])
    tri = sb("tri", [P, P])
    causal = sb("causal", [P, P])
    xz = sb("xz", [P, KD, T])
    ps = ctx.enter_context(nc.psum_tensor("ps", [P, 8, 512], F32))

    one = ExitStack()
    gate_ffn_row = sb("gate_ffn_row", [P, D], scope=one)
    acc = sb("acc", [P, D], scope=one)
    mixer = ExitStack()
    hH = sb("hH", [P, KD, T], F32R, mixer)
    hL = sb("hL", [P, KD, T], F32R, mixer)
    wH = sb("wH", [P, 3, D], F32R, mixer)
    wL = sb("wL", [P, 3, D], F32R, mixer)
    gate_c = sb("gate_c", [P, T], scope=mixer)
    cv = sb("cv", [P, T + 2], scope=mixer)
    vtmp = sb("vtmp", [P, 2, 512], scope=mixer)
    mixer.close()
    outp = ExitStack()
    woH = sb("woH", [P, KD, D], F32R, outp)
    woL = sb("woL", [P, KD, D], F32R, outp)
    zsH = sb("zsH", [P, 2, KD, P], F32R, outp)
    zsL = sb("zsL", [P, 2, KD, P], F32R, outp)
    xt = sb("xt", [P, 2, D], scope=outp)
    h2t = sb("h2t", [P, D], scope=outp)
    h2T = sb("h2T", [P, KD, P], scope=outp)
    gate_row = sb("gate_row", [P, D], scope=outp)
    gain_row = sb("gain_row", [P, D], scope=outp)
    shift_row = sb("shift_row", [P, D], scope=outp)
    outp.close()
    moe = ExitStack()
    lg1 = sb("lg1", [P, NT, E1], scope=moe)
    aff = sb("aff", [P, NT, E1], scope=moe)
    smax = sb("smax", [P, 4, NT], scope=moe)
    affT = sb("affT", [E1, 2, T], scope=moe)
    top_v = sb("top_v", [E1, CAP1], scope=moe)
    top_i = sb("top_i", [E1, CAP1], U32, moe)
    top_f = sb("top_f", [E1, CAP1], scope=moe)
    slot_gate = sb("slot_gate", [P, E1], scope=moe)
    slot_tok = sb("slot_tok", [P, E1], U32, moe)
    tok_in = [sb(f"tok_in{u}", [P, 1], U32, moe) for u in range(2)]
    tok_out = [sb(f"tok_out{u}", [P, 1], U32, moe) for u in range(2)]
    mH = sb("mH", [P, WSETS, D], F32R, moe)
    mL = sb("mL", [P, WSETS, D], F32R, moe)
    xsH = sb("xsH", [P, 2, KD, P], F32R, moe)
    xsL = sb("xsL", [P, 2, KD, P], F32R, moe)
    hidH = sb("hidH", [P, KD, P], F32R, moe)
    hidL = sb("hidL", [P, KD, P], F32R, moe)
    lg2 = sb("lg2", [P, NT, NR2], scope=moe)
    sel2 = sb("sel2", [P, 2, NT, 8], scope=moe)
    cand = sb("cand", [P, NT, 8], scope=moe)
    hot4 = sb("hot4", [P, NT, 4], scope=moe)
    hot8 = sb("hot8", [P, 2, NT, 8], scope=moe)
    hot32 = sb("hot32", [P, 3, NT, E2], scope=moe)
    slotm = sb("slotm", [P, 2, NT, E2], scope=moe)
    r2 = sb("r2", [P, 12, NT], scope=moe)
    cnt = sb("cnt", [P, 8, E2], scope=moe)
    slot_u = sb("slot_u", [P, 2, NT], U32, moe)
    tokid = sb("tokid", [P, NT], U32, moe)
    tok_rows = sb("tok_rows", [NBLK, P], U32, moe)
    tok_rows_f = sb("tok_rows_f", [NBLK, P], scope=moe)
    tokc = sb("tokc", [P, NBLK], U32, moe)
    iota_b = sb("iota_b", [P, NOVF], scope=moe)
    oblk = sb("oblk", [P, NOVF, E2], scope=moe)
    oexp = sb("oexp", [P, NOVF], scope=moe)
    oexp_u = sb("oexp_u", [P, NOVF + 1], U32, moe)
    final_row = sb("final_row", [P, D], scope=moe)
    otok = sb("otok", [P, 1], U32, moe)
    oxT = sb("oxT", [P, KD, P], scope=moe)
    ohT = sb("ohT", [P, 4, P], scope=moe)
    moe.close()
    one.close()
    two = ExitStack()
    vt = sb("vt", [P, NT, 4, P + 1], scope=two)
    og2 = sb("og2", [P, 2, T], scope=two)
    tA = sb("tA", [P, T], scope=two)
    tB = sb("tB", [P, T], scope=two)
    negM = sb("negM", [4, T], scope=two)
    gt = sb("gt", [P, NT, 8], scope=two)
    gcol = sb("gcol", [P, 2, NT, 4], scope=two)
    invc = sb("invc", [P, 4, 16], scope=two)
    edge = sb("edge", [P, 16], scope=two)
    proj = ExitStack()
    gH = sb("gH", [P, KD, T], F32R, proj)
    gL = sb("gL", [P, KD, T], F32R, proj)
    uH = sb("uH", [P, 2, D], F32R, proj)
    uL = sb("uL", [P, 2, D], F32R, proj)
    proj.close()
    cell = ExitStack()
    wq = sb("wq", [P, 4, P], scope=cell)
    wk = sb("wk", [P, 4, P], scope=cell)
    wp = sb("wp", [P, 4, P], scope=cell)
    qT = sb("qT", [P, 2, T], scope=cell)
    kT = sb("kT", [P, 2, T], scope=cell)
    mB = sb("mB", [P, 2, T], scope=cell)
    wt = sb("wt", [P, 2, T], scope=cell)
    pm = sb("pm", [P, 2, NT * (NT + 1) // 2 * P], scope=cell)
    num = sb("num", [P, NT, P + 1], scope=cell)
    dtmp = sb("dtmp", [P, 2, P], scope=cell)
    pick = sb("pick", [4, 4, P], scope=cell)
    ms = sb("ms", [P, 8, NT], scope=cell)
    cell.close()
    two.close()
    og = [tA[:], tB[:], og2[:, 0, :], og2[:, 1, :]]
    sq = ring[:, 0, :]
    sk = ring[:, 1, :]
    xs = [xz[:, u, :] for u in range(2)]
    ys = [xz[:, 2 + u, :] for u in range(2)]
    sg = xz[:, 4, :]
    hid = xz[:, 5, :]

    S = {}
    for name in SEMS.split():
        S[name] = ctx.enter_context(nc.semaphore(name))

    lines = [
        [("x1_done", NT), ("x1_done_2", NT), ("x_final", NT)],
        [("sq2", NT), ("sq2_2", NT), ("sq_final", NT)],
        [("var2", NT), ("var2_2", NT), ("var_final", NT)],
        [("rstd2", NT), ("rstd2_2", NT), ("rstd_final", NT)],
        [("diag_used", 4 * KD), ("diag_used_2", 4 * KD)],
        [("diag_ready", 4 * KD), ("diag_ready_2", 4 * KD)],
        [("h2_out", 16 * NT), ("h2_out_2", 16 * NT)],
        [("bc_done", 4), ("bc_done_2", 4)],
        [("var_ready", 1), ("var_ready_2", 1), ("hv_ready", 4)],
        [("rstd_ready", 1), ("rstd_ready_2", 1), ("hr_ready", 4)],
        [("split_done", 4 * KD), ("d2_split", 3 * KD)],
        [("split_hi", 4 * KD), ("d2_hi", 3 * KD)],
        [("f_part", 3 * KD), ("d2_part", 16)],
        [("m1_used", 24 * E1), ("m2_used", 12 * E2), ("ov_gu", NOVF)],
        [("m1_hi", 24 * E1), ("m2_hi", 12 * E2)],
        [("m1_lo", 24 * E1), ("m2_lo", 12 * E2)],
        [("m1_tok", E1), ("m2_tok", E2), ("ov_tok", NOVF)],
        [("m1_xT", 2 * E1), ("m2_xT", 2 * E2), ("ov_xT", NOVF)],
        [("m1_xT_hi", 2 * E1), ("m2_xT_hi", 2 * E2), ("ov_x", NOVF)],
        [("m1_xT_lo", 2 * E1), ("m2_xT_lo", 2 * E2)],
        [("m1_silu", 2 * E1), ("m2_silu", E2), ("ov_silu", NOVF)],
        [("m1_hid", 2 * E1), ("m2_hid", E2), ("ov_hid", NOVF)],
        [("m1_hT", 2 * E1), ("m2_hT", E2), ("ov_hT", NOVF)],
        [("m1_hT_hi", 2 * E1), ("m2_hT_hi", E2), ("ov_h", NOVF)],
        [("m1_hT_lo", 2 * E1), ("m2_hT_lo", E2)],
        [("m2_y", E2), ("ov_y", NOVF)],
        [("gt_ready", 1), ("gate_in", 1), ("gate_rows", 2), ("gate_m", 1), ("neg_ready", 1), ("gcol_ready", 2)],
        [("gate_exp", 1), ("gate_ln", 1), ("floor", 1)],
        [("if_mm", 1), ("gt_tr", 1), ("gate_cols", 1)],
        [("masks", 5), ("ones_col", 1), ("counts", 5), ("pick", 2), ("route_consts", 4)],
        [("tok_zero", 16), ("tok_set", 32 * NT), ("tok_back", 16)],
        [("route1", 1), ("route2_a", 1), ("route2_b", 1)],
        [("e1_exp", 1), ("route2_exp", 2)],
        [("aff_ready", 1), ("top_ready", 1), ("hot_ready", 1), ("tok_f", 1)],
        [("affT_tr", 1), ("topT_tr", 1), ("ranks", 1), ("tok_tr", 1)],
        [("slots_ready", 1), ("slots2", 2), ("ov_known", 1)],
        [("final_in", 16), ("ov_stored", 16 * NOVF)],
        [("rows_zero", 1), ("cols_ready", 1)],
        [("sq_done", NT), ("sq_done_2", NT)],
        [("xn_done", NT), ("xn_done_2", NT)],
    ]
    lines += [[(name, NT), (name + "_2", NT)]
              for name in ("h2_done", "y_ready", "zs_hi", "zs_lo", "h2T_ready", "rt_done")]
    lines += [[("tr2", NT), ("tr2_2", NT), ("ov_down", NOVF)]]
    lines += [[(name, 2 * KD), (name + "_2", 2 * KD)] for name in ("tr_ready", "tr_hi", "tr_lo")]
    past = {}
    for line in lines:
        done = 0
        for name, count in line:
            S[name] = S[line[0][0]]
            past[name], done = done, done + count

    def sems(name, n):
        return [ctx.enter_context(nc.semaphore(f"{name}{s}")) for s in range(n)]

    ring_in = sems("ring_in", RING)
    x_in = sems("x_in", NT)
    xs_in, y_added = sems("xs_in", 2), sems("y_added", 2)
    m2_out = y_added
    xt_in, x1_out = sems("xt_in", 2), sems("x1_out", 2)
    c_in, c_out = sems("c_in", 2), sems("c_out", 2)
    XT_PAST = {"": 0, "_2": 16 * NT // 2}
    XS_PAST = 16 * E1 // 2

    block = ctx.enter_context(nc.Block())

    SPLITS1, ADAS1 = 3 * KD + KD, 2 * KD + 4 * KD + 6 * KD
    used1 = [-(-(SPLITS1 - s) // SPLIT_RING) for s in range(SPLIT_RING)]
    used1 += [-(-(ADAS1 - s) // ADA_RING) for s in range(ADA_RING)] + [0, 0]

    def split_landed(eng, q, m):
        eng.wait_ge(ring_in[m % SPLIT_RING], 16 * (q + m // SPLIT_RING + 1))

    def ada_landed(eng, q, a):
        eng.wait_ge(ring_in[SPLIT_RING + a % ADA_RING], 16 * (q + a // ADA_RING + 1))

    def m1_landed(eng, e, c):
        eng.wait_ge(ring_in[c % RING], 16 * (used1[c % RING] + 2 * e + c // RING + 1))

    def settle(eng):
        eng.sem_inc(S["wait_passed"])

    def static(q):
        return isinstance(q, int)

    def m1_waits(q, r, m):
        return not (static(q) and 2 * q + r == 0 and m < WSETS)

    w_in1 = io["sc_w_in"].rearrange("(k p) n -> p k n", p=P)
    w_out1 = io["sc_w_out"].rearrange("(k p) n -> p k n", p=P)
    ada1 = io["ada_w"].rearrange("(k p) n -> p k n", p=P)
    ada2 = io["ada_w_2"].rearrange("(k p) n -> p k n", p=P)
    moe_g, moe_u, moe_d = (io[n].rearrange("e (k p) n -> e p k n", p=P)
                           for n in ("moe_w_gate", "moe_w_up", "moe_w_down"))
    x_tiles = io["x"].rearrange("(t p) d -> p t d", p=P)
    x1_tiles = x1_dram.rearrange("(t p) d -> p t d", p=P)
    h2_tiles = h2_dram.rearrange("(t p) d -> p t d", p=P)

    w_in2, w_out2 = (io[n].rearrange("(k p) n -> p k n", p=P) for n in ("w_in_2", "w_out_2"))
    m2_g, m2_u, m2_d = (io[n].rearrange("e (k p) n -> e p k n", p=P)
                        for n in ("w_expert_gate_2", "w_expert_up_2", "w_expert_down_2"))
    x3_tiles = x3_dram.rearrange("(t p) d -> p t d", p=P)
    h4_tiles = h4_dram.rearrange("(t p) d -> p t d", p=P)
    tok_blocks = tok_dram.rearrange("(b p) o -> b (p o)", p=P)
    yslot_blocks = yslot_dram.rearrange("(b p) d -> p b d", p=P)
    FIRST_O, FIRST_P = 2 * F2, 3 * F2 + 8
    WINDOWS = (2, 4, 8, 16)

    used2 = [u + 2 * E1 + 2 for u in used1]

    def m2_at(q, r, c):
        if static(q):
            s = 2 * q + r
            n = c if s == 0 else 12 * s - 4 + c - (8 if s == E2 else 0)
            return n, n % RING, n % WSETS, n // RING
        n = 12 * r - 4 + c
        return 24 * q + n, n % RING, n % WSETS, 2 * q + n // RING

    def m2_steps(eng, body):
        for r in range(2):
            body(0, r)
        with eng.Fori(1, E2 // 2 - 1) as q:
            for r in range(2):
                body(q, r)
        for s in range(E2 - 2, E2 + 1):
            body(s // 2, s % 2)

    def overflow_blocks(eng, overflow):
        eng.wait_ge(S["ov_known"], 1 + past["ov_known"])
        blocks = eng.value_load(oexp_u[0:1, NOVF:NOVF + 1], min_val=0, max_val=NOVF)
        with eng.If(blocks > 0):
            with eng.Fori(0, NOVF) as b:
                with eng.If(blocks > b):
                    overflow(b)
        return blocks

    row_at = [{}, {}]
    at = [0, 0]
    for b, name, n in ((0, "c", 8), (0, "c_2", 8), (0, "ada_b", 48), (0, "norm_g", 16), (0, "norm1_g_2", 8),
                       (0, "norm2_g_2", 8), (0, "sc_conv", 24), (1, "ada_b_2", 48), (1, "conv_w_2", 16),
                       (1, "conv_b_2", 4), (1, "mlstm_norm_g_2", 4), (1, "mlstm_skip_2", 4), (1, "b_pool_2", 4),
                       (1, "pool_scale_2", 4), (1, "final_g_2", 8)):
        row_at[b][name] = (at[b], n)
        at[b] += n

    def col(name, j, n=1):
        b = 0 if name in row_at[0] else 1
        return cols[:, b, bass.ds(row_at[b][name][0] + j, n)]

    @block.sync
    def _(sp):
        def ada_chunk(src, q, a, k, j, first=False):
            if not first:
                sp.wait_ge(S["ada_done"], 4 * q + a - ADA_RING + 1)
                if not static(q):
                    settle(sp)
            sp.dma_start(ring[:, SPLIT_RING + a % ADA_RING, :],
                         src[:, k, bass.ds(D * j, D)]).then_inc(ring_in[SPLIT_RING + a % ADA_RING], 16)

        def split_chunk(src, q, m, n, first=False):
            if not first:
                sp.wait_ge(S["split_done"], 6 * q + m - SPLIT_RING + 1)
                if not static(q):
                    settle(sp)
            slot = ring[:, m % SPLIT_RING, :]
            sp.dma_start(slot.rearrange("p (k n) -> p k n", n=n) if n < D else slot,
                         src).then_inc(ring_in[m % SPLIT_RING], 16)

        def in_chunks(q, r):
            for p, part in enumerate((1, 2, 0)):
                split_chunk(w_in1[:, :, bass.ds((2 * q + r) * P + part * D, P)], q, 3 * r + p, P,
                            first=static(q) and q == 0)

        for a in range(4):
            ada_chunk(ada1, 0, a, a % KD, a // KD, first=True)
        in_chunks(0, 0)
        for a in range(4, 16):
            ada_chunk(ada1, 0, a, a % KD, a // KD)

        def f_step(q, r):
            for c in range(4):
                ada_chunk(ada1, 2 * q + r + 4, c, 4 * r + c, q + 2)
            if r == 0:
                in_chunks(q, 1)
            elif not (static(q) and q == 3):
                in_chunks(q + 1, 0)

        in_pairs(sp, KD, f_step)
        for k in range(KD):
            split_chunk(w_out1[:, k, :], 4, k, D)

        def output_stage(b, residual):
            def o_step(q, r):
                s = 2 * q + r
                if not (static(q) and s == NT):
                    if not (static(q) and s < 2):
                        sp.wait_ge(x1_out[r], 16 * q + XT_PAST[b])
                        if not static(q):
                            settle(sp)
                        sp.wait_ge(S["h2_done" + b], s - 1 + past["h2_done" + b])
                        if not static(q):
                            settle(sp)
                    sp.dma_start(xt[:, r, :], residual[:, s, :]).then_inc(xt_in[r], 16)
                if b == "" and (not static(q) or 1 <= s <= 6):
                    for c in range(8):
                        ada_chunk(ada2, 4 * q + 2 * r + 10, c, c, s - 1)

            in_pairs(sp, NT + 1, o_step)

        sp.wait_ge(S["z_done"], KD)
        output_stage("", x_tiles)

        def m1_step(q, r):
            e = 2 * q + r
            for c in range(24):
                s = c % RING
                if static(q) and e == 0 and c < RING:
                    if s < SPLIT_RING:
                        sp.wait_ge(S["split_done"], s + 1 + SPLIT_RING * (used1[s] - 1))
                    elif s < SPLIT_RING + ADA_RING:
                        sp.wait_ge(S["ada_done"], s - SPLIT_RING + 1 + ADA_RING * (used1[s] - 1))
                else:
                    sp.wait_ge(S["m1_lo"], 24 * e + c - RING + 1)
                    if not static(q):
                        settle(sp)
                if c < 16:
                    n, kp = c // 8, (c % 8) // 2
                    src = (moe_g, moe_u)[c % 2][e, :, 2 * kp:2 * kp + 2, 512 * n:512 * n + 512]
                    dst = ring[:, s, :].rearrange("p (k n) -> p k n", k=2)
                else:
                    src, dst = moe_d[e, :, c - 16, :], ring[:, s, :]
                sp.dma_start(dst, src).then_inc(ring_in[s], 16)

        in_pairs(sp, E1, m1_step)

        def d2_chunk(m, src, n):
            s = m % RING
            if m < RING:
                sp.wait_ge(S["m1_lo"], 24 * E1 - RING + m + 1)
            else:
                sp.wait_ge(S["d2_split"], m - RING + 1 + past["d2_split"])
            slot = ring[:, s, :]
            sp.dma_start(slot.rearrange("p (k n) -> p k n", n=n) if n < D else slot, src).then_inc(ring_in[s], 16)

        for m in range(4):
            d2_chunk(m, w_in2[:, 2 * m:2 * m + 2, F2:2 * F2], F2)
        for m in range(4, 16):
            first = (0, FIRST_P, FIRST_O)[(m - 4) // 4] + (m % 4) * P
            d2_chunk(m, w_in2[:, :, first:first + P], P)
        for k in range(KD):
            d2_chunk(16 + k, w_out2[:, k, :], D)
        sp.wait_ge(S["hy_done"], 4)
        sp.wait_ge(S["pool_out"], 4)
        sp.wait_ge(S["unused_zero"], 16 * NOVF)
        output_stage("_2", x1_tiles)

        def m2_chunk(q, r, c):
            n, slot, _, _ = m2_at(q, r, c)
            s = 2 * q + r
            if static(q) and n < RING:
                sp.wait_ge(S["d2_split"], RING + n + 1 + past["d2_split"])
            else:
                sp.wait_ge(S["m2_lo"], n - RING + 1 + past["m2_lo"])
                if not static(q):
                    settle(sp)
            if c < 8:
                src = (m2_g, m2_u)[c % 2][s, :, 2 * (c // 2):2 * (c // 2) + 2, :]
                dst = ring[:, slot, :].rearrange("p (k n) -> p k n", k=2)
            else:
                src, dst = m2_d[s - 1, :, c - 8, :], ring[:, slot, :]
            sp.dma_start(dst, src).then_inc(ring_in[slot], 16)

        def m2_step(q, r):
            s = 2 * q + r
            for c in range(12):
                if not (static(q) and (s == 0 and c >= 8 or s == E2 and c < 8)):
                    m2_chunk(q, r, c)

        m2_steps(sp, m2_step)

        def overflow(b):
            e = sp.value_load(oexp_u[0:1, bass.ds(b, 1)], min_val=0, max_val=E2 - 1)
            for c in range(12):
                if c < 8:
                    sp.wait_ge(S["ov_gu"], b + past["ov_gu"])
                else:
                    sp.wait_ge(S["ov_down"], b + past["ov_down"])
                settle(sp)
                if c < 8:
                    src = (m2_g, m2_u)[c % 2][e, :, 2 * (c // 2):2 * (c // 2) + 2, :]
                    dst = ring[:, c, :].rearrange("p (k n) -> p k n", k=2)
                else:
                    src, dst = m2_d[e, :, c - 8, :], ring[:, c, :]
                sp.dma_start(dst, src).then_inc(ring_in[c], 16)

        sp.wait_ge(S["m2_y"], E2)
        overflow_blocks(sp, overflow)

        for t in range(NT):
            sp.wait_ge(S["final_done"], t + 1)
            sp.dma_start(out.rearrange("(t p) d -> p t d", p=P)[:, t, :], ring[:, 6 + t % 2, :]).then_inc(c_out[t % 2], 16)
        for u in range(2):
            sp.wait_ge(c_out[u], 16 * NT // 2)

    @block.gpsimd
    def _(pool):
        pool.memset(ones[:], 1.0).then_inc(S["consts"], 1)
        pool.memset(ident[:], 0.0).then_inc(S["consts"], 1)
        pool.memset(neghalf[:], -0.5).then_inc(S["consts"], 1)
        pool.wait_ge(S["consts"], 3)
        pool.affine_select(out=ident[:], in_=ident[:], compare_op=ALU.not_equal, fill=1.0, base=0,
                           pattern=[[-1, P]], channel_multiplier=1).then_inc(S["consts"], 1)
        pool.iota(iota8[:], [[1, 8]], base=0, channel_multiplier=0,
                  allow_small_or_imprecise_dtypes=True).then_inc(S["masks"], 1)
        pool.memset(tri[:], 1.0).then_inc(S["masks"], 1)
        pool.memset(causal[:], 0.0).then_inc(S["masks"], 1)
        pool.wait_ge(S["masks"], 3)
        pool.affine_select(out=tri[:], in_=tri[:], compare_op=ALU.is_gt, fill=0.0, base=0,
                           pattern=[[1, P]], channel_multiplier=-1).then_inc(S["masks"], 1)
        pool.affine_select(out=causal[:], in_=causal[:], compare_op=ALU.is_ge, fill=-1e30, base=0,
                           pattern=[[1, P]], channel_multiplier=-1).then_inc(S["masks"], 1)
        pool.wait_ge(S["var_ready"], 1)
        pool.tensor_tensor(stat[:, 2, :], stat[:, 1, :], neghalf[:], ALU.pow).then_inc(S["rstd_ready"], 1)

        def output_stage(b, residual_out, normed_out):
            def o_step(q, r):
                s = 2 * q + r
                if static(q) and s == NT:
                    return
                pool.wait_ge(S["x1_done" + b], s + 1 + past["x1_done" + b])
                if not static(q):
                    settle(pool)
                pool.dma_start(residual_out[:, s, :], xt[:, r, :]).then_inc(x1_out[r], 16)
                pool.wait_ge(S["var2" + b], s + 1 + past["var2" + b])
                pool.tensor_tensor(stat[:, 6, 0:1], stat[:, 5, 0:1], neghalf[:, 0:1], ALU.pow).then_inc(S["rstd2" + b], 1)
                pool.wait_ge(S["h2_done" + b], s + 1 + past["h2_done" + b])
                if not static(q):
                    settle(pool)
                pool.dma_start(normed_out[:, s, :], h2t[:]).then_inc(S["h2_out" + b], 16)
                pool.wait_ge(S["h2_out" + b], 16 * s + 16 + past["h2_out" + b])

            in_pairs(pool, NT + 1, o_step)
            for u in range(2):
                pool.wait_ge(x1_out[u], 16 * NT // 2 + XT_PAST[b])
            pool.sem_inc(S["stored"], 1)

        output_stage("", x1_tiles, h2_tiles)

        def gather(q, r):
            e = 2 * q + r
            pool.wait_ge(S["m1_tok"], e + 1)
            if not static(q):
                settle(pool)
            pool.indirect_dma_start(out=xs[r], out_offset=None, in_=h2_dram,
                                    in_offset=bass.IndirectOffsetOnAxis(ap=tok_in[r][:, 0:1], axis=0)
                                    ).then_inc(xs_in[r], 16)

        def add_rows(q, r):
            e = 2 * q + r
            pool.wait_ge(S["m1_y_done"], e + 1)
            pool.wait_ge(y_added[1 - r], 16 * q + 16 * r)
            if not static(q):
                settle(pool)
            pool.indirect_dma_start(out=x1_dram, in_=ys[r], in_offset=None, compute_op=ALU.add,
                                    out_offset=bass.IndirectOffsetOnAxis(ap=tok_out[r][:, 0:1], axis=0)
                                    ).then_inc(y_added[r], 16)

        gather(0, 0)

        def m1_step(q, r):
            if not (static(q) and 2 * q + r == E1 - 1):
                gather(q, 1) if r == 0 else gather(q + 1, 0)
            if not (static(q) and 2 * q + r == 0):
                add_rows(q, 0) if r == 1 else add_rows(q - 1, 1)

        in_pairs(pool, E1, m1_step)
        add_rows(E1 // 2 - 1, 1)
        for u in range(2):
            pool.wait_ge(y_added[u], 16 * E1 // 2)

        pool.wait_ge(S["sq_done_2"], NT + past["sq_done_2"])
        pool.memset(vt[:, :, :, P:P + 1], 1.0).then_inc(S["ones_col"], 1)
        pool.iota(invc[:], [[0, 4], [1, 16]], base=1, channel_multiplier=0,
                  allow_small_or_imprecise_dtypes=True).then_inc(S["counts"], 1)
        pool.wait_ge(S["counts"], 1 + past["counts"])
        for g in range(4):
            pool.tensor_scalar(invc[:, g, :], invc[:, g, :], float(WINDOWS[g]), None, ALU.min).then_inc(S["counts"], 1)
        pool.wait_ge(S["var_ready_2"], 1 + past["var_ready_2"])
        pool.tensor_tensor(stat[:, 2, :], stat[:, 1, :], neghalf[:], ALU.pow).then_inc(S["rstd_ready_2"], 1)
        pool.wait_ge(S["d2_part"], 16 + past["d2_part"])
        pool.wait_ge(S["d2_split"], 16 + past["d2_split"])
        pool.memset(pick[:], 0.0).then_inc(S["pick"], 1)
        pool.wait_ge(S["pick"], 1 + past["pick"])
        pool.affine_select(out=pick[:], in_=pick[:], compare_op=ALU.not_equal, fill=1.0, base=0,
                           pattern=[[-1, 4], [0, P]], channel_multiplier=1).then_inc(S["pick"], 1)
        pool.memset(ring[:, 2, :], 0.0).then_inc(S["zero_row"], 1)
        pool.wait_ge(S["zero_row"], 1)
        for b in range(NOVF):
            pool.dma_start(yslot_blocks[:, E2 + b, :], ring[:, 2, :]).then_inc(S["unused_zero"], 16)
        for h in range(4):
            pool.wait_ge(S["hv_ready"], h + 1 + past["hv_ready"])
            pool.tensor_tensor(ms[:, 4, :], ms[:, 3, :], neghalf[:], ALU.pow).then_inc(S["hr_ready"], 1)
        pool.wait_ge(S["unused_zero"], 16 * NOVF)
        output_stage("_2", x3_tiles, h4_tiles)

        pool.wait_ge(S["rt_done_2"], NT + past["rt_done_2"])
        pool.iota(tokid[:], [[P, NT]], base=0, channel_multiplier=1).then_inc(S["route_consts"], 1)
        pool.iota(iota_b[:], [[1, NOVF]], base=0, channel_multiplier=0,
                  allow_small_or_imprecise_dtypes=True).then_inc(S["route_consts"], 1)
        pool.iota(cnt[:, 6, :], [[P, E2]], base=0, channel_multiplier=0,
                  allow_small_or_imprecise_dtypes=True).then_inc(S["route_consts"], 1)
        pool.memset(tok_rows[:], 0).then_inc(S["route_consts"], 1)
        pool.wait_ge(S["route_consts"], 4 + past["route_consts"])
        pool.dma_start(tok_blocks, tok_rows[:]).then_inc(S["tok_zero"], 16)
        pool.wait_ge(S["tok_zero"], 16)
        pool.wait_ge(S["slots2"], 2 + past["slots2"])
        for i in range(2):
            for t in range(NT):
                pool.indirect_dma_start(out=tok_dram, in_=tokid[:, t:t + 1], in_offset=None,
                                        out_offset=bass.IndirectOffsetOnAxis(ap=slot_u[:, i, t:t + 1], axis=0)
                                        ).then_inc(S["tok_set"], 16)
        pool.wait_ge(S["tok_set"], 32 * NT + past["tok_set"])
        pool.dma_start(tok_rows[:], tok_blocks).then_inc(S["tok_back"], 16)
        for u in range(2):
            pool.wait_ge(x1_out[u], 16 * NT // 2 + XT_PAST["_2"])

        def gather2(q, r):
            e = 2 * q + r
            pool.wait_ge(S["m2_tok"], e + 1 + past["m2_tok"])
            if not static(q):
                settle(pool)
            pool.indirect_dma_start(out=xs[r], out_offset=None, in_=h4_dram,
                                    in_offset=bass.IndirectOffsetOnAxis(ap=tok_in[r][:, 0:1], axis=0)
                                    ).then_inc(xs_in[r], 16)

        def store_y(q, r):
            e = 2 * q + r
            pool.wait_ge(S["m2_y"], e + 1)
            if not static(q):
                settle(pool)
            pool.dma_start(yslot_blocks[:, e, :], ys[r]).then_inc(m2_out[r], 16)

        gather2(0, 0)
        gather2(0, 1)

        def m2_step(q, r):
            s = 2 * q + r
            if not (static(q) and s + 2 >= E2):
                gather2(q + 1, r)
            if not (static(q) and s < 2):
                store_y(q - 1, r)

        m2_steps(pool, m2_step)
        store_y(E2 // 2 - 1, 1)
        for u in range(2):
            pool.wait_ge(m2_out[u], 16 * E2 // 2 + XS_PAST)

        def overflow(b):
            pool.wait_ge(S["ov_tok"], b + 1 + past["ov_tok"])
            settle(pool)
            pool.indirect_dma_start(out=xs[0], out_offset=None, in_=h4_dram,
                                    in_offset=bass.IndirectOffsetOnAxis(ap=otok[:, 0:1], axis=0)
                                    ).then_inc(xs_in[0], 16)

        overflow_blocks(pool, overflow)
        pool.wait_ge(S["ov_over"], 1)

        def gather_rows(t):
            if t >= 2:
                pool.wait_ge(S["final_done"], t - 1)
            for i in range(2):
                pool.indirect_dma_start(out=ring[:, 2 * i + t % 2, :], out_offset=None, in_=yslot_dram,
                                        in_offset=bass.IndirectOffsetOnAxis(ap=slot_u[:, i, t:t + 1], axis=0)
                                        ).then_inc(c_in[t % 2], 16)
            pool.dma_start(ring[:, 4 + t % 2, :], x3_tiles[:, t, :]).then_inc(c_in[t % 2], 16)

        gather_rows(0)
        for t in range(NT):
            if t < NT - 1:
                gather_rows(t + 1)
            pool.wait_ge(S["var_final"], t + 1 + past["var_final"])
            pool.tensor_tensor(stat[:, 10, 0:1], stat[:, 9, 0:1], neghalf[:, 0:1], ALU.pow).then_inc(S["rstd_final"], 1)

    @block.scalar
    def _(act):
        act.wait_ge(S["rows_zero"], 1)
        for b in range(2):
            for name, (first, n) in row_at[b].items():
                act.dma_start(rows[first:first + n, b, :], io[name]).then_inc(S["rows_in"], 16)
        for t in range(NT):
            act.dma_start(xz[:, t, :], x_tiles[:, t, :]).then_inc(x_in[t], 16)
        act.dma_start(router1[:], io["moe_router"].rearrange("(k p) n -> p k n", p=P)).then_inc(S["small_in"], 16)
        b_groups, b_experts = (io[n].rearrange("a b -> (a b)").partition_broadcast(P)
                               for n in ("b_router_group_2", "b_router_expert_2"))
        for dst, src in ((w_if[:], w_in2[:, :, 3 * F2:3 * F2 + 8]),
                         (router2[:, :, 0:4], io["w_router_group_2"].rearrange("(k p) n -> p k n", p=P)),
                         (router2[:, :, 4:NR2], io["w_router_expert_2"].rearrange("(k p) n -> p k n", p=P)),
                         (bias2[:, 0:4], b_groups), (bias2[:, 4:NR2], b_experts),
                         (gbias[:, 0:1], io["b_igate_2"]), (gbias[:, 1:2], io["b_fgate_2"])):
            act.dma_start(dst, src).then_inc(S["small_in"], 16)
        act.wait_ge(S["cols_ready"], 1 + past["cols_ready"])
        act.activation(silu_c[:], cols[:, 0, 0:16], ACT.Silu).then_inc(S["silu_ready"], 1)
        for t in range(NT):
            act.wait_ge(x_in[t], 16)
            if t:
                act.wait_ge(S["sq_done"], t)
            act.activation(gate_c[:], xz[:, t, :], ACT.Square,
                           accum_out=stat[:, 0, t:t + 1]).then_inc(S["sq_done"], 1)
        act.wait_ge(S["mod_ready"], 3)
        for g in range(16):
            half, c = g // KD, g % KD
            act.wait_ge(S["tr_ready"], g + 1)
            act.activation(hH[:, c, half * 512:half * 512 + 512], ps[:, g % 4, :], ACT.Identity,
                           bias=mod[:, 0, c:c + 1], scale=gain[:, 0, c:c + 1]).then_inc(S["tr_hi"], 1)

        def split_hi(q, m, dst, freed=None):
            split_landed(act, q, m)
            if freed is not None:
                act.wait_ge(*freed)
            act.activation(dst, ring[:, m % SPLIT_RING, :], ACT.Copy).then_inc(S["split_hi"], 1)

        def in_splits(q, r):
            for p in range(3):
                m = 3 * r + p
                first = static(q) and q == 0 and m < 3
                split_hi(q, m, wH[:, p, :], None if first else (S["f_part"], 6 * q + m - 2))

        in_splits(0, 0)

        def f_step(q, r):
            f = 2 * q + r
            act.wait_ge(S["f_part"], 3 * f + 1)
            if not (static(q) and f == 0):
                act.wait_ge(S["cv_done"], f)
            act.activation(gate_c[:].rearrange("p (a b) -> p a b", a=2), ps[:, 0:2, :],
                           ACT.Copy).then_inc(S["c_copied"], 1)
            if r == 0:
                in_splits(q, 1)
            elif not (static(q) and q == 3):
                in_splits(q + 1, 0)

        in_pairs(act, KD, f_step)
        act.wait_ge(S["z_done"], KD)
        for k in range(KD):
            split_hi(4, k, woH[:, k, :], (S["f_part"], 3 * KD) if k == 0 else None)

        def output_stage(b):
            rows_to = (gate_row, gain_row, shift_row, gate_ffn_row)
            for n, dst in enumerate(rows_to):
                act.wait_ge(S["diag_used" + b], 8 * n + 8 + past["diag_used" + b])
                act.activation(dst[:].rearrange("p (a b) -> p a b", a=2), ps[:, 2 * (n % 2):2 * (n % 2) + 2, :],
                               ACT.Copy).then_inc(S["bc_done" + b], 1)

            def token_slice(q, r):
                t = 2 * q + r
                if not (static(q) and t < 2):
                    act.wait_ge(S["y_ready" + b], t - 1 + past["y_ready" + b])
                act.activation(zsH[:, r, :, :], xz[:, :, bass.ds(t * P, P)], ACT.Copy).then_inc(S["zs_hi" + b], 1)

            token_slice(0, 0)

            def o_step(q, r):
                s = 2 * q + r
                if not (static(q) and s >= NT - 1):
                    token_slice(q, 1) if r == 0 else token_slice(q + 1, 0)
                if not (static(q) and s == 0):
                    act.wait_ge(S["tr2" + b], s + past["tr2" + b])
                    act.activation(h2T[:].rearrange("p (a b) c -> p a (b c)", a=2), ps[:, 4:6, :],
                                   ACT.Copy).then_inc(S["h2T_ready" + b], 1)
                if not (static(q) and s == NT):
                    act.wait_ge(S["x1_done" + b], s + 1 + past["x1_done" + b])
                    act.activation(h2t[:], xt[:, r, :], ACT.Square, accum_out=stat[:, 4, 0:1]).then_inc(S["sq2" + b], 1)

            in_pairs(act, NT + 1, o_step)

        output_stage("")

        act.wait_ge(S["route1"], 1)
        act.activation(aff[:], lg1[:], ACT.Exp).then_inc(S["e1_exp"], 1)

        def m1_split(e, m, waits):
            m1_landed(act, e, m)
            if waits:
                act.wait_ge(S["m1_used"], 24 * e + m - WSETS + 1)
            act.activation(mH[:, m % WSETS, :], ring[:, m % RING, :], ACT.Copy).then_inc(S["m1_hi"], 1)

        def x_hi(e, r, j):
            act.wait_ge(S["m1_xT"], 2 * e + j + 1)
            act.activation(xsH[:, r, 4 * j:4 * j + 4, :].rearrange("p a b -> p (a b)"), ps[:, 6 + j, :],
                           ACT.Copy).then_inc(S["m1_xT_hi"], 1)

        act.wait_ge(S["slots_ready"], 1)
        for j in range(2):
            x_hi(0, 0, j)

        def m1_step(q, r):
            e = 2 * q + r
            for m in range(24):
                if m == 13 or m == 21:
                    n = m // 21
                    act.wait_ge(S["m1_used"], 24 * e + 8 * n + 8)
                    act.activation(sg[:, 512 * n:512 * n + 512], ps[:, n, :], ACT.Silu).then_inc(S["m1_silu"], 1)
                if m == 19 or m == 22:
                    j = m // 22
                    act.wait_ge(S["m1_hT"], 2 * e + j + 1)
                    act.activation(hidH[:, 4 * j:4 * j + 4, :].rearrange("p a b -> p (a b)"), ps[:, 2 * j, :],
                                   ACT.Copy).then_inc(S["m1_hT_hi"], 1)
                if m == 21 and not (static(q) and e == E1 - 1):
                    for j in range(2):
                        x_hi(e + 1, 1 - r, j)
                m1_split(e, m, m1_waits(q, r, m))

        in_pairs(act, E1, m1_step)

        for u in range(2):
            act.wait_ge(y_added[u], 16 * E1 // 2)
        for t in range(NT):
            act.dma_start(xz[:, t, :], x1_tiles[:, t, :]).then_inc(x_in[t], 16)
        for t in range(NT):
            act.wait_ge(x_in[t], 32)
            if t:
                act.wait_ge(S["sq_done_2"], t + past["sq_done_2"])
            act.activation(tB[:], xz[:, t, :], ACT.Square, accum_out=stat[:, 0, t:t + 1]).then_inc(S["sq_done_2"], 1)
        act.wait_ge(S["small_in"], 16 * 8)
        act.activation(w_ifH[:], w_if[:], ACT.Copy).then_inc(S["if_hi"], 1)
        for g in range(16):
            half, c = g // KD, g % KD
            act.wait_ge(S["tr_ready_2"], g + 1 + past["tr_ready_2"])
            act.activation(gH[:, c, half * 512:half * 512 + 512], ps[:, g % 4, :], ACT.Identity,
                           bias=mod[:, 1, c:c + 1], scale=gain[:, 2, c:c + 1]).then_inc(S["tr_hi_2"], 1)

        def d2_hi(m):
            act.wait_ge(ring_in[m % RING], 16 * (used1[m % RING] + 2 * E1 + m // RING + 1))
            if 2 <= m < 16:
                act.wait_ge(S["d2_part"], m - 1 + past["d2_part"])
            dst = uH[:, m % 2, :] if m < 16 else woH[:, m - 16, :]
            act.activation(dst, ring[:, m % RING, :], ACT.Copy).then_inc(S["d2_hi"], 1)

        for m in range(4):
            d2_hi(m)
        for t in range(0, NT, 2):
            act.wait_ge(S["d2_part"], 4 + past["d2_part"])
            act.activation(vt[:, t, :, 0:P], ps[:, t, :].rearrange("p (h d) -> p h d", h=4),
                           ACT.Copy).then_inc(S["v_even"], 1)
        d2_hi(4)
        f_abs, thr = xz[0:4, 6, :], xz[0:4, 6, :]

        def gates():
            act.wait_ge(S["gate_rows"], 2 + past["gate_rows"])
            act.activation(f_abs, f_abs, ACT.Exp, scale=-1.0).then_inc(S["gate_exp"], 1)
            act.wait_ge(S["gate_exp"], 1)
            act.activation(f_abs, f_abs, ACT.Ln, bias=1.0).then_inc(S["gate_ln"], 1)

        def floor():
            act.wait_ge(S["gate_m"], 1 + past["gate_m"])
            act.activation(thr, xz[0:4, 5, :], ACT.Exp, scale=-1.0).then_inc(S["floor"], 1)

        for i in range(12):
            m, pair = 4 + i, ps[:, 2 * (i % 4):2 * (i % 4) + 2, :]
            if i < 11:
                d2_hi(m + 1)
            act.wait_ge(S["d2_part"], m + 1 + past["d2_part"])
            if i < 8:
                if i:
                    act.wait_ge(S["branch"], i)
                act.activation(tA[:].rearrange("p (a b) -> p a b", a=2), pair, ACT.Copy).then_inc(S["d2_out"], 1)
            else:
                act.wait_ge(S["branch"], 8)
                act.activation(og[i - 8].rearrange("p (a b) -> p a b", a=2), pair, ACT.Sigmoid).then_inc(S["d2_out"], 1)
            if i == 0:
                gates()
            if i < 4:
                act.wait_ge(S["branch"], i + 1)
                act.activation(xz[:, i, :], xz[:, i, :], ACT.Silu, bias=col("conv_b_2", i)).then_inc(S["uc_ready"], 1)
            if i == 2:
                floor()
        act.wait_ge(S["d2_part"], 16 + past["d2_part"])
        act.wait_ge(S["d2_split"], 16 + past["d2_split"])
        for dst, name in ((wq, "w_q_2"), (wk, "w_k_2"), (wp, "w_pool_2")):
            act.dma_start(dst[:], io[name].rearrange("h d e -> d h e")).then_inc(S["cell_in"], 16)

        def pair_copy(dst, src, sem, scale=1.0):
            act.activation(dst.rearrange("p (a b) -> p a b", a=2), src, ACT.Copy, scale=scale).then_inc(S[sem], 1)

        def head_scores(h):
            act.wait_ge(S["q_mm"], h + 1)
            pair_copy(qT[:, h % 2, :], ps[:, 4:6, :], "q_out", P ** -0.5)
            act.wait_ge(S["m_mm"], h + 1)
            pair_copy(mB[:, h % 2, :], ps[:, 4:6, :], "m_out")
            for s in range(NT):
                i = NT * h + s
                act.wait_ge(S["dmask"], i + 1)
                if i >= 2:
                    act.wait_ge(S["pm_ready"], i - 1)
                act.wait_ge(S["m_out"], h + 1)
                act.activation(wt[:, i % 2, 0:P], dtmp[:, i % 2, :], ACT.Exp).then_inc(S["wt_diag"], 1)
                if s < NT - 1:
                    act.activation(wt[:, i % 2, P:T - P * s], mB[:, h % 2, P * (s + 1):T], ACT.Exp,
                                   bias=gcol[:, 0, s, h:h + 1]).then_inc(S["wt_rest"], 1)

        head_scores(0)
        for h in range(4):
            if h < 3:
                head_scores(h + 1)
            for t in range(NT):
                act.wait_ge(S["pv"], NT * h + t + 1)
                if t == 0 and h:
                    act.wait_ge(S["hn_tr"], h)
                act.activation(num[:, t, :], ps[:, 6 + t % 2, 0:P + 1], ACT.Copy).then_inc(S["num_out"], 1)
        act.wait_ge(S["hy_done"], 4)
        act.wait_ge(S["pool_out"], 4)
        for m in range(16, 24):
            d2_hi(m)
        output_stage("_2")

        act.wait_ge(S["route2_a"], 1 + past["route2_a"])
        act.activation(cand[:, :, 0:4], cand[:, :, 0:4], ACT.Exp).then_inc(S["route2_exp"], 1)
        act.wait_ge(S["route2_b"], 1 + past["route2_b"])
        act.activation(r2[:, 5, :], r2[:, 5, :], ACT.Exp).then_inc(S["route2_exp"], 1)
        act.dma_start(final_row[:], io["final_g_2"].rearrange("a b -> (a b)").partition_broadcast(P)
                      ).then_inc(S["final_in"], 16)

        def m2_hi(q, r, c):
            n, slot, wset, turn = m2_at(q, r, c)
            act.wait_ge(ring_in[slot], 16 * (used2[slot] + turn + 1))
            if not (static(q) and n < WSETS):
                act.wait_ge(S["m2_used"], n - WSETS + 1 + past["m2_used"])
            act.activation(mH[:, wset, :], ring[:, slot, :], ACT.Copy).then_inc(S["m2_hi"], 1)

        def x_hi2(e, r, j):
            act.wait_ge(S["m2_xT"], 2 * e + j + 1 + past["m2_xT"])
            act.activation(xsH[:, r, 4 * j:4 * j + 4, :].rearrange("p a b -> p (a b)"), ps[:, 7 - j, :],
                           ACT.Copy).then_inc(S["m2_xT_hi"], 1)

        def y_copy(q, r):
            e = 2 * q + r
            act.wait_ge(S["m2_used"], (12 * e + 20 if not (static(q) and e == E2 - 1) else 12 * E2) + past["m2_used"])
            act.wait_ge(m2_out[r], 16 * q + XS_PAST)
            act.activation(ys[r].rearrange("p (a b) -> p a b", a=2), ps[:, 4:6, :], ACT.Copy).then_inc(S["m2_y"], 1)

        for j in range(2):
            x_hi2(0, 0, j)

        def m2_step(q, r):
            s = 2 * q + r
            for c in range(12):
                if static(q) and s == 0 and c >= 8:
                    break
                if c == 1 and not (static(q) and s == 0):
                    act.wait_ge(S["m2_used"], (8 if static(q) and s == 1 else 12 * s - 8) + past["m2_used"])
                    act.activation(sg[:, 512 * (1 - r):512 * (1 - r) + 512], ps[:, 2 * (1 - r), :],
                                   ACT.Silu).then_inc(S["m2_silu"], 1)
                if c == 6 and not (static(q) and s < 2):
                    y_copy(q - 1, r)
                if c == 8:
                    act.wait_ge(S["m2_hT"], s + past["m2_hT"])
                    act.activation(hidH[:, 0:4, :].rearrange("p a b -> p (a b)"), ps[:, 6, :],
                                   ACT.Copy).then_inc(S["m2_hT_hi"], 1)
                if c in (9, 11) and not (static(q) and s >= E2 - 1):
                    x_hi2(s + 1, 1 - r, (c - 9) // 2)
                if not (static(q) and s == E2 and c < 8):
                    m2_hi(q, r, c)
            if static(q) and s == 0:
                for j in range(2):
                    x_hi2(1, 1, j)

        m2_steps(act, m2_step)
        y_copy((E2 - 1) // 2, 1)

        act.wait_ge(m2_out[0], 16 * (E2 // 2) + XS_PAST)

        def overflow(b):
            act.wait_ge(S["ov_xT"], b + 1 + past["ov_xT"])
            act.activation(oxT[:].rearrange("p (a b) c -> p a (b c)", a=2), ps[:, 6:8, :],
                           ACT.Copy).then_inc(S["ov_x"], 1)
            act.wait_ge(S["ov_gu"], b + 1 + past["ov_gu"])
            act.activation(sg[:, 0:512], ps[:, 0, :], ACT.Silu).then_inc(S["ov_silu"], 1)
            act.wait_ge(S["ov_hT"], b + 1 + past["ov_hT"])
            act.activation(ohT[:].rearrange("p a b -> p (a b)"), ps[:, 6, :], ACT.Copy).then_inc(S["ov_h"], 1)
            act.wait_ge(S["ov_down"], b + 1 + past["ov_down"])
            act.wait_ge(S["ov_stored"], 16 * b + past["ov_stored"])
            act.activation(ys[0].rearrange("p (a b) -> p a b", a=2), ps[:, 4:6, :], ACT.Copy).then_inc(S["ov_y"], 1)
            act.wait_ge(S["ov_y"], b + 1 + past["ov_y"])
            settle(act)
            act.dma_start(yslot_blocks[:, b + E2, :], ys[0]).then_inc(S["ov_stored"], 16)

        blocks = overflow_blocks(act, overflow)
        act.wait_ge(S["ov_stored"], 16 * blocks + past["ov_stored"])
        settle(act)
        act.sem_inc(S["ov_over"], 1)

        for t in range(NT):
            act.wait_ge(S["x_final"], t + 1 + past["x_final"])
            act.activation(ring[:, 2 + t % 2, :], ring[:, 4 + t % 2, :], ACT.Square,
                           accum_out=stat[:, 8, 0:1]).then_inc(S["sq_final"], 1)

    @block.vector
    def _(dve):
        steps = Steps(dve, S["dve_steps"])
        dve.memset(rows[:], 0.0).then_inc(S["rows_zero"], 1)
        dve.wait_ge(S["cols_tr"], 2)
        dve.tensor_copy(cols[:], ps[:, 7, 0:2 * P].rearrange("p (a b) -> p a b", a=2)).then_inc(S["cols_ready"], 1)
        steps.mark(dve.memset(cv[:], 0.0))

        def ada_sum(q, a, k, first, silu_col):
            ada_landed(dve, q, a)
            slot = ring[:, SPLIT_RING + a % ADA_RING, :]
            if first:
                ins = dve.tensor_scalar(acc[:], slot, silu_c[:, silu_col + k:silu_col + k + 1], None, ALU.mult)
            else:
                dve.wait_ge(S["ada_done"], 4 * q + a)
                ins = dve.scalar_tensor_tensor(out=acc[:], in0=slot, scalar=silu_c[:, silu_col + k:silu_col + k + 1],
                                               in1=acc[:], op0=ALU.mult, op1=ALU.add)
            ins.then_inc(S["ada_done"], 1)

        dve.wait_ge(S["silu_ready"], 1)
        for a in range(KD):
            ada_sum(0, a, a, a == 0, 0)
        dve.wait_ge(S["sq_done"], NT)
        dve.tensor_scalar(stat[:, 1, :], stat[:, 0, :], 1.0 / D, EPS, ALU.mult, ALU.add).then_inc(S["var_ready"], 1)
        for a in range(KD, 2 * KD):
            if a == KD:
                dve.wait_ge(S["mod_mm"], 1)
            ada_sum(0, a, a - KD, a == KD, 0)
        dve.wait_ge(S["rstd_ready"], 1)
        for t in range(NT):
            dve.tensor_scalar(xz[:, t, :], xz[:, t, :], stat[:, 2, t:t + 1], None, ALU.mult).then_inc(S["xn_done"], 1)
        dve.wait_ge(S["mod_mm"], 2)
        dve.tensor_tensor(mod[:, 0, 0:16], ps[:, 7, 256:272], col("ada_b", 0, 16), ALU.add).then_inc(S["mod_ready"], 1)
        dve.wait_ge(S["mod_ready"], 1)
        dve.tensor_scalar(gain[:, 0, :], mod[:, 0, 8:16], 1.0, None, ALU.add).then_inc(S["mod_ready"], 1)
        dve.wait_ge(S["mod_ready"], 2)
        dve.tensor_tensor(gain[:, 0, :], gain[:, 0, :], col("norm_g", 0, 8), ALU.mult).then_inc(S["mod_ready"], 1)
        dve.wait_ge(S["mod_ready"], 3)
        for g in range(16):
            half, c = g // KD, g % KD
            dve.wait_ge(S["tr_hi"], g + 1)
            if g >= 2:
                dve.wait_ge(S["tr_lo"], g - 1)
            steps.mark(dve.tensor_scalar(vtmp[:, g % 2, :], ps[:, g % 4, :], gain[:, 0, c:c + 1], mod[:, 0, c:c + 1],
                                         ALU.mult, ALU.add))
            steps.wait()
            at_g = (slice(None), c, slice(half * 512, half * 512 + 512))
            dve.tensor_tensor(hL[at_g], vtmp[:, g % 2, :], hH[at_g].bitcast(F32), ALU.subtract).then_inc(S["tr_lo"], 1)

        def split_lo(q, m, high, dst):
            dve.wait_ge(S["split_hi"], 6 * q + m + 1)
            dve.tensor_tensor(dst, ring[:, m % SPLIT_RING, :], high.bitcast(F32),
                              ALU.subtract).then_inc(S["split_done"], 1)

        for p in range(3):
            split_lo(0, p, wH[:, p, :], wL[:, p, :])

        def f_step(q, r):
            f = 2 * q + r
            last = static(q) and f == KD - 1
            nq, nr = (q, 1) if r == 0 else (q + 1, 0)
            dve.wait_ge(S["f_part"], 3 * f + 2)
            dve.wait_ge(S["c_copied"], f + 1)
            steps.wait()
            dve.tensor_tensor(cv[:, 1:T + 1].rearrange("p (a b) -> p a b", a=2), ps[:, 2:4, :],
                              gate_c[:].rearrange("p (a b) -> p a b", a=2), ALU.mult).then_inc(S["cv_done"], 1)
            dve.wait_ge(S["cv_done"], f + 1)
            z = xz[:, f, :]
            steps.mark(dve.tensor_scalar(z, cv[:, 0:T], col("sc_conv", f), None, ALU.mult))
            for tap in (1, 2):
                steps.wait()
                steps.mark(dve.scalar_tensor_tensor(out=z, in0=cv[:, tap:tap + T], scalar=col("sc_conv", f + 8 * tap),
                                                    in1=z, op0=ALU.mult, op1=ALU.add))
            if not last:
                for p in range(2):
                    split_lo(nq, 3 * nr + p, wH[:, p, :], wL[:, p, :])
            for c in range(4):
                if r == 0 and c == 0:
                    dve.wait_ge(S["mod_mm"], q + 2)
                ada_sum(2 * q + r + 4, c, 4 * r + c, r == 0 and c == 0, 0)
            dve.wait_ge(S["f_part"], 3 * f + 3)
            z2 = z.rearrange("p (a b) -> p a b", a=2)
            dve.tensor_tensor(z2, z2, ps[:, 4:6, :], ALU.mult).then_inc(S["z_done"], 1)
            if not last:
                split_lo(nq, 3 * nr + 2, wH[:, 2, :], wL[:, 2, :])

        in_pairs(dve, KD, f_step, steps, 6)
        for k in range(KD):
            split_lo(4, k, woH[:, k, :], woL[:, k, :])

        def mod_columns(b, first, n, name, number):
            dve.tensor_tensor(mod[:, b, first:first + n], ps[:, 7, 256 + 48 * b + first:256 + 48 * b + first + n],
                              col(name, first, n), ALU.add).then_inc(S["mod_ready"], 1)
            dve.wait_ge(S["mod_ready"], number)

        def gain_columns(g, b, scale_at, name, name_at, number):
            dve.tensor_scalar(gain[:, g, :], mod[:, b, scale_at:scale_at + 8], 1.0, None,
                              ALU.add).then_inc(S["mod_ready"], 1)
            dve.wait_ge(S["mod_ready"], number)
            dve.tensor_tensor(gain[:, g, :], gain[:, g, :], col(name, name_at, 8), ALU.mult).then_inc(S["mod_ready"], 1)
            dve.wait_ge(S["mod_ready"], number + 1)

        dve.wait_ge(S["mod_mm"], 6)
        mod_columns(0, 16, 32, "ada_b", 4)
        gain_columns(1, 0, 32, "norm_g", 8, 5)

        def output_stage(b, sources):
            for n, source in enumerate(sources):
                for c in range(KD):
                    if 8 * n + c >= 2:
                        dve.wait_ge(S["diag_used" + b], 8 * n + c - 1 + past["diag_used" + b])
                    dve.tensor_scalar(diag[:, c % 2, :], ident[:], source[:, c:c + 1], None,
                                      ALU.mult).then_inc(S["diag_ready" + b], 1)

            def slice_lo(q, r):
                t = 2 * q + r
                dve.wait_ge(S["zs_hi" + b], t + 1 + past["zs_hi" + b])
                dve.tensor_tensor(zsL[:, r, :, :], xz[:, :, bass.ds(t * P, P)], zsH[:, r, :, :].bitcast(F32),
                                  ALU.subtract).then_inc(S["zs_lo" + b], 1)

            slice_lo(0, 0)
            dve.wait_ge(S["bc_done" + b], len(sources) + past["bc_done" + b])

            def o_step(q, r):
                s = 2 * q + r
                if not (static(q) and s >= NT - 1):
                    slice_lo(q, 1) if r == 0 else slice_lo(q + 1, 0)
                if b == "" and (not static(q) or 1 <= s <= 6):
                    for c in range(8):
                        if c == 0:
                            dve.wait_ge(S["mod_mm"], s + 5)
                        ada_sum(4 * q + 2 * r + 10, c, c, c == 0, 8)
                if static(q) and s == NT:
                    return
                dve.wait_ge(S["y_ready" + b], s + 1 + past["y_ready" + b])
                if not (static(q) and s == 0):
                    dve.wait_ge(S["tr2" + b], s + past["tr2" + b])
                    dve.wait_ge(S["h2_out" + b], 16 * s + past["h2_out" + b])
                h2t2, gate2 = (a[:].rearrange("p (a b) -> p a b", a=2) for a in (h2t, gate_row))
                steps.mark(dve.tensor_tensor(h2t2, ps[:, 2 * r:2 * r + 2, :], gate2, ALU.mult))
                dve.wait_ge(xt_in[r], 16 * q + 16 + XT_PAST[b])
                steps.wait()
                dve.tensor_tensor(xt[:, r, :], xt[:, r, :], h2t[:], ALU.add).then_inc(S["x1_done" + b], 1)
                dve.wait_ge(S["sq2" + b], s + 1 + past["sq2" + b])
                dve.tensor_scalar(stat[:, 5, 0:1], stat[:, 4, 0:1], 1.0 / D, EPS, ALU.mult,
                                  ALU.add).then_inc(S["var2" + b], 1)
                dve.wait_ge(S["rstd2" + b], s + 1 + past["rstd2" + b])
                steps.mark(dve.scalar_tensor_tensor(out=h2t[:], in0=xt[:, r, :], scalar=stat[:, 6, 0:1],
                                                    in1=gain_row[:], op0=ALU.mult, op1=ALU.mult))
                steps.wait()
                dve.tensor_tensor(h2t[:], h2t[:], shift_row[:], ALU.add).then_inc(S["h2_done" + b], 1)

            in_pairs(dve, NT + 1, o_step, steps, 4)

        output_stage("", (mod[:, 0, 16:24], gain[:, 1, :], mod[:, 0, 24:32], mod[:, 0, 40:48]))
        dve.wait_ge(S["mod_mm"], 12)
        mod_columns(1, 0, 48, "ada_b_2", 7)
        gain_columns(2, 1, 8, "norm1_g_2", 0, 8)
        gain_columns(3, 1, 32, "norm2_g_2", 0, 10)

        def step(ins):
            steps.mark(ins)
            steps.wait()

        dve.wait_ge(S["rt_done"], NT)
        dve.wait_ge(S["stored"], 1)
        step(dve.tensor_copy(lg1[:].rearrange("p t e -> p (t e)"), ps[:, 6, 0:NT * E1]))
        step(dve.tensor_reduce(smax[:, 0, :], lg1[:], AX, ALU.max))

        def by_expert(v, n=E1):
            return v.unsqueeze(2).to_broadcast([P, NT, n])

        dve.tensor_tensor(lg1[:], lg1[:], by_expert(smax[:, 0, :]), ALU.subtract).then_inc(S["route1"], 1)
        dve.wait_ge(S["e1_exp"], 1)
        step(dve.tensor_reduce(smax[:, 1, :], aff[:], AX, ALU.add))
        step(dve.reciprocal(smax[:, 2, :], smax[:, 1, :]))
        dve.tensor_tensor(aff[:], aff[:], by_expert(smax[:, 2, :]), ALU.mult).then_inc(S["aff_ready"], 1)
        dve.wait_ge(S["affT_tr"], 1)
        step(dve.tensor_copy(affT[:, 0, :].rearrange("p (a b) -> p a b", a=2), ps[0:E1, 0:2, :]))
        for i in range(CAP1 // 8):
            best = slice(8 * i, 8 * i + 8)
            step(dve.max(top_v[:, best], affT[:, i % 2, :]))
            step(dve.max_index(top_i[:, best], top_v[:, best], affT[:, i % 2, :]))
            if i < CAP1 // 8 - 1:
                step(dve.match_replace(affT[:, 1 - i % 2, :], top_v[:, best], affT[:, i % 2, :], -1.0))
        dve.tensor_copy(top_f[:], top_i[:]).then_inc(S["top_ready"], 1)
        dve.wait_ge(S["topT_tr"], 1 + past["topT_tr"])
        step(dve.tensor_copy(slot_gate[:], ps[:, 2, 0:E1]))
        dve.tensor_copy(slot_tok[:], ps[:, 2, E1:2 * E1]).then_inc(S["slots_ready"], 1)
        dve.wait_ge(S["slots_ready"], 1)

        def m1_split(e, m):
            dve.wait_ge(S["m1_hi"], 24 * e + m + 1)
            dve.tensor_tensor(mL[:, m % WSETS, :], ring[:, m % RING, :], mH[:, m % WSETS, :].bitcast(F32),
                              ALU.subtract).then_inc(S["m1_lo"], 1)

        def x_lo(e, r, j):
            dve.wait_ge(S["m1_xT_hi"], 2 * e + j + 1)
            part = xsH[:, r, 4 * j:4 * j + 4, :].rearrange("p a b -> p (a b)")
            dve.tensor_tensor(xsL[:, r, 4 * j:4 * j + 4, :].rearrange("p a b -> p (a b)"), ps[:, 6 + j, :],
                              part.bitcast(F32), ALU.subtract).then_inc(S["m1_xT_lo"], 1)

        def tokens(e, r, src):
            dve.tensor_copy(tok_in[r][:], slot_tok[:, bass.ds(e, 1)]).then_inc(S["m1_tok"], 1)

        tokens(0, 0, 0)
        for j in range(2):
            x_lo(0, 0, j)

        def y_out(q, r):
            e = 2 * q + r
            dve.wait_ge(S["m1_used"], 24 * e + 24)
            dve.wait_ge(y_added[r], 16 * q)
            steps.mark(dve.tensor_copy(tok_out[r][:], slot_tok[:, bass.ds(e, 1)]))
            dve.scalar_tensor_tensor(out=ys[r].rearrange("p (a b) -> p a b", a=2), in0=ps[:, 4:6, :],
                                     scalar=slot_gate[:, bass.ds(e, 1)],
                                     in1=gate_ffn_row[:].rearrange("p (a b) -> p a b", a=2),
                                     op0=ALU.mult, op1=ALU.mult).then_inc(S["m1_y_done"], 1)

        def m1_step(q, r):
            e = 2 * q + r
            for m in range(24):
                if m == 1 and not (static(q) and e == E1 - 1):
                    if not (static(q) and e == 0):
                        dve.wait_ge(S["m1_xT"], 2 * e)
                    tokens(e + 1, 1 - r, 0)
                if m == 6 and not (static(q) and e == 0):
                    y_out(q, 0) if r == 1 else y_out(q - 1, 1)
                if m == 13 or m == 21:
                    n = m // 21
                    dve.wait_ge(S["m1_silu"], 2 * e + n + 1)
                    dve.tensor_tensor(hid[:, 512 * n:512 * n + 512], sg[:, 512 * n:512 * n + 512], ps[:, 2 + n, :],
                                      ALU.mult).then_inc(S["m1_hid"], 1)
                if m == 19 or m == 22:
                    j = m // 22
                    dve.wait_ge(S["m1_hT_hi"], 2 * e + j + 1)
                    part = hidH[:, 4 * j:4 * j + 4, :].rearrange("p a b -> p (a b)")
                    dve.tensor_tensor(hidL[:, 4 * j:4 * j + 4, :].rearrange("p a b -> p (a b)"), ps[:, 2 * j, :],
                                      part.bitcast(F32), ALU.subtract).then_inc(S["m1_hT_lo"], 1)
                if m == 21 and not (static(q) and e == E1 - 1):
                    for j in range(2):
                        x_lo(e + 1, 1 - r, j)
                m1_split(e, m)

        in_pairs(dve, E1, m1_step, steps, 2)
        y_out(E1 // 2 - 1, 1)

        dve.wait_ge(S["sq_done_2"], NT + past["sq_done_2"])
        dve.tensor_scalar(stat[:, 1, :], stat[:, 0, :], 1.0 / D, EPS, ALU.mult, ALU.add).then_inc(S["var_ready_2"], 1)
        dve.wait_ge(S["rstd_ready_2"], 1 + past["rstd_ready_2"])
        for t in range(NT):
            dve.tensor_scalar(xz[:, t, :], xz[:, t, :], stat[:, 2, t:t + 1], None, ALU.mult).then_inc(S["xn_done_2"], 1)
        dve.wait_ge(S["if_hi"], 1)
        dve.tensor_tensor(w_ifL[:], w_if[:], w_ifH[:].bitcast(F32), ALU.subtract).then_inc(S["if_lo"], 1)
        for g in range(16):
            half, c = g // KD, g % KD
            tmp = tA[:, (g % 2) * 512:(g % 2) * 512 + 512]
            dve.wait_ge(S["tr_hi_2"], g + 1 + past["tr_hi_2"])
            if g >= 2:
                dve.wait_ge(S["tr_lo_2"], g - 1 + past["tr_lo_2"])
            step(dve.tensor_scalar(tmp, ps[:, g % 4, :], gain[:, 2, c:c + 1], mod[:, 1, c:c + 1], ALU.mult, ALU.add))
            at_g = (slice(None), c, slice(half * 512, half * 512 + 512))
            dve.tensor_tensor(gL[at_g], tmp, gH[at_g].bitcast(F32), ALU.subtract).then_inc(S["tr_lo_2"], 1)

        def d2_lo(m):
            high, dst = (uH[:, m % 2, :], uL[:, m % 2, :]) if m < 16 else (woH[:, m - 16, :], woL[:, m - 16, :])
            dve.wait_ge(S["d2_hi"], m + 1 + past["d2_hi"])
            dve.tensor_tensor(dst, ring[:, m % RING, :], high.bitcast(F32), ALU.subtract).then_inc(S["d2_split"], 1)

        for m in range(4):
            d2_lo(m)
        for t in range(1, NT, 2):
            dve.wait_ge(S["d2_part"], 4 + past["d2_part"])
            dve.tensor_copy(vt[:, t, :, 0:P], ps[:, t, :].rearrange("p (h d) -> p h d", h=4)).then_inc(S["v_odd"], 1)
        d2_lo(4)
        dve.wait_ge(S["if_mm"], 1)
        dve.tensor_copy(gt[:].rearrange("p t g -> p (t g)"), ps[:, 7, 0:8 * NT]).then_inc(S["gt_ready"], 1)

        g_in, g_forget, g_abs, g_sum = (xz[0:4, 4 + i, :] for i in range(4))

        def gate_inputs():
            dve.wait_ge(S["gt_tr"], 1 + past["gt_tr"])
            dve.tensor_scalar(g_in.rearrange("p (a b) -> p a b", a=2), ps[0:4, 4:6, :], gbias[:, 0:1], None,
                              ALU.add).then_inc(S["gate_in"], 1)
            dve.tensor_scalar(g_forget.rearrange("p (a b) -> p a b", a=2), ps[0:4, 6:8, :], gbias[:, 1:2], None,
                              ALU.add).then_inc(S["gate_rows"], 1)
            dve.wait_ge(S["gate_rows"], 1 + past["gate_rows"])
            dve.scalar_tensor_tensor(out=g_abs, in0=g_forget, scalar=-1.0, in1=g_forget, op0=ALU.mult,
                                     op1=ALU.max).then_inc(S["gate_rows"], 1)

        def gate_scans():
            dve.wait_ge(S["gate_ln"], 1 + past["gate_ln"])
            step(dve.scalar_tensor_tensor(out=g_forget, in0=g_forget, scalar=0.0, in1=g_abs, op0=ALU.min,
                                          op1=ALU.subtract))
            step(dve.memset(g_abs, 1.0))
            step(dve.tensor_tensor_scan(g_sum, g_abs, g_forget, 0.0, ALU.mult, ALU.add))
            step(dve.tensor_tensor(g_in, g_in, g_sum, ALU.subtract))
            step(dve.tensor_tensor_scan(negM[:], g_in, g_in, 0.0, ALU.max, ALU.max))
            dve.tensor_tensor(g_forget, g_sum, negM[:], ALU.add).then_inc(S["gate_m"], 1)
            dve.wait_ge(S["gate_m"], 1 + past["gate_m"])
            dve.tensor_scalar(negM[:], negM[:], -1.0, None, ALU.mult).then_inc(S["neg_ready"], 1)

        def conv_branch(i):
            dve.wait_ge(S["d2_out"], i + 1)
            step(dve.tensor_scalar(xz[:, i, :], tA[:], col("conv_w_2", 12 + i), None, ALU.mult))
            for back in (1, 2, 3):
                ins = dve.scalar_tensor_tensor(out=xz[:, i, back:T], in0=tA[:, 0:T - back],
                                               scalar=col("conv_w_2", 4 * (3 - back) + i), in1=xz[:, i, back:T],
                                               op0=ALU.mult, op1=ALU.add)
                if back < 3:
                    step(ins)
                else:
                    ins.then_inc(S["branch"], 1)

        def pool_branch(g):
            own, dst = tA[:], xz[:, 4 + g, :]
            dve.wait_ge(S["d2_out"], 5 + g)
            src, span = own, 1
            while span < WINDOWS[g]:
                to = tB[:] if span in (1, 4) else dst
                steps.mark(dve.tensor_copy(to[:, 0:span], src[:, 0:span]))
                step(dve.tensor_tensor(to[:, span:T], src[:, span:T], src[:, 0:T - span], ALU.add))
                src, span = to, 2 * span
            step(dve.tensor_tensor(edge[:], src[:, 0:16], invc[:, g, :], ALU.mult))
            step(dve.scalar_tensor_tensor(out=dst, in0=src, scalar=1.0 / WINDOWS[g], in1=own, op0=ALU.mult,
                                          op1=ALU.subtract))
            dve.tensor_tensor(dst[:, 0:16], edge[:], own[:, 0:16], ALU.subtract).then_inc(S["branch"], 1)

        for i in range(12):
            if i < 11:
                d2_lo(5 + i)
            if i == 0:
                gate_inputs()
            if i < 4:
                conv_branch(i)
            elif i < 8:
                pool_branch(i - 4)
            if i == 0:
                gate_scans()
                dve.wait_ge(S["counts"], 5 + past["counts"])
                step(dve.reciprocal(invc[:], invc[:]))
            if i == 3:
                dve.wait_ge(S["gate_cols"], 1 + past["gate_cols"])
                for j in range(2):
                    src = ps[:, 0, 32 * j:32 * j + 32].rearrange("p (t h) -> p t h", h=4)
                    dve.tensor_copy(gcol[:, j, :, :], src).then_inc(S["gcol_ready"], 1)

        for g in range(4):
            dve.wait_ge(S["pool_mm"], g + 1)
            dve.tensor_scalar(xz[:, 4 + g, :].rearrange("p (a b) -> p a b", a=2), ps[:, 2 * (g % 2):2 * (g % 2) + 2, :],
                              col("b_pool_2", g), col("pool_scale_2", g), ALU.add, ALU.mult).then_inc(S["pool_out"], 1)

        offs = [P * sum(NT - j for j in range(s)) for s in range(NT)]

        def head_scores(h):
            dve.wait_ge(S["k_mm"], h + 1)
            dve.tensor_copy(kT[:, h % 2, :].rearrange("p (a b) -> p a b", a=2), ps[:, 6:8, :]).then_inc(S["k_out"], 1)
            dve.wait_ge(S["m_out"], h + 1)

            def diagonal(s):
                i = NT * h + s
                if i >= 2:
                    dve.wait_ge(S["wt_diag"], i - 1)
                dve.scalar_tensor_tensor(out=dtmp[:, i % 2, :], in0=mB[:, h % 2, P * s:P * s + P],
                                         scalar=gcol[:, 0, s, h:h + 1], in1=causal[:], op0=ALU.add,
                                         op1=ALU.add).then_inc(S["dmask"], 1)

            diagonal(0)
            for s in range(NT):
                i, n = NT * h + s, T - P * s
                if s < NT - 1:
                    diagonal(s + 1)
                dve.wait_ge(S["s_mm"], i + 1)
                dve.wait_ge(S["wt_diag"], i + 1)
                dve.wait_ge(S["wt_rest"], 7 * h + min(s + 1, 7))
                pair = ps[:, 2 * (i % 2):2 * (i % 2) + 2, :].rearrange("p a b -> p (a b)")
                dve.tensor_tensor(pm[:, h % 2, offs[s]:offs[s] + n], pair[:, 0:n], wt[:, i % 2, 0:n],
                                  ALU.mult).then_inc(S["pm_ready"], 1)

        def head_norm(h):
            dve.wait_ge(S["num_out"], NT * h + NT)
            sq3 = sq.rearrange("p (t d) -> p t d", t=NT)
            step(dve.scalar_tensor_tensor(out=ms[:, 0, :], in0=num[:, :, P], scalar=-1.0, in1=num[:, :, P],
                                          op0=ALU.mult, op1=ALU.max))
            step(dve.tensor_tensor(ms[:, 1, :], ms[:, 0, :], gcol[:, 1, :, h], ALU.max))
            steps.mark(dve.reciprocal(ms[:, 2, :], ms[:, 1, :]))
            step(dve.tensor_tensor(sq3, num[:, :, 0:P], num[:, :, 0:P], ALU.mult))
            steps.mark(dve.tensor_reduce(ms[:, 5, :], sq3, AX, ALU.add))
            step(dve.tensor_tensor(ms[:, 6, :], ms[:, 2, :], ms[:, 2, :], ALU.mult))
            step(dve.tensor_tensor(ms[:, 6, :], ms[:, 6, :], ms[:, 5, :], ALU.mult))
            dve.tensor_scalar(ms[:, 3, :], ms[:, 6, :], 1.0 / P, EPS, ALU.mult, ALU.add).then_inc(S["hv_ready"], 1)
            steps.mark(dve.tensor_scalar(sk, xz[:, h, :], col("mlstm_skip_2", h), None, ALU.mult))
            dve.wait_ge(S["hr_ready"], h + 1 + past["hr_ready"])
            step(dve.tensor_tensor(ms[:, 7, :], ms[:, 2, :], ms[:, 4, :], ALU.mult))
            dve.tensor_tensor(num[:, :, 0:P], num[:, :, 0:P], by_expert(ms[:, 7, :], P),
                              ALU.mult).then_inc(S["hn_ready"], 1)
            dve.wait_ge(S["hn_tr"], h + 1)
            sk2 = sk.rearrange("p (a b) -> p a b", a=2)
            step(dve.scalar_tensor_tensor(out=sk2, in0=ps[:, 4:6, :], scalar=col("mlstm_norm_g_2", h), in1=sk2,
                                          op0=ALU.mult, op1=ALU.add))
            dve.tensor_tensor(xz[:, h, :], sk, og[h], ALU.mult).then_inc(S["hy_done"], 1)

        dve.wait_ge(S["masks"], 5)
        head_scores(0)
        for h in range(4):
            if h < 3:
                head_scores(h + 1)
            head_norm(h)
        for m in range(16, 24):
            d2_lo(m)
        output_stage("_2", (mod[:, 1, 16:24], gain[:, 3, :], mod[:, 1, 24:32], mod[:, 1, 40:48]))

        dve.wait_ge(S["rt_done_2"], NT + past["rt_done_2"])
        dve.wait_ge(S["stored"], 2)
        dve.wait_ge(S["small_in"], 16 * 8)
        g_logit, best, top, second = lg2[:, :, 0:4], r2[:, 0, :], r2[:, 3, :], r2[:, 4, :]
        step(dve.tensor_tensor(lg2[:], ps[:, 6, 0:NT * NR2].rearrange("p (t n) -> p t n", t=NT),
                               bias2[:].unsqueeze(1).to_broadcast([P, NT, NR2]), ALU.add))
        step(dve.tensor_reduce(best, g_logit, AX, ALU.max))
        dve.tensor_tensor(cand[:, :, 0:4], g_logit, by_expert(best, 4), ALU.subtract).then_inc(S["route2_a"], 1)

        def first_hot(dst, v, m, n):
            step(dve.tensor_tensor(dst, v, by_expert(m, n), ALU.is_equal))
            step(dve.scalar_tensor_tensor(out=dst, in0=dst, scalar=-8.0,
                                          in1=iota8[:, 0:n].unsqueeze(1).to_broadcast([P, NT, n]),
                                          op0=ALU.mult, op1=ALU.add))
            step(dve.tensor_reduce(r2[:, 6, :], dst, AX, ALU.min))
            step(dve.tensor_tensor(dst, dst, by_expert(r2[:, 6, :], n), ALU.is_equal))

        first_hot(hot4[:], g_logit, best, 4)
        step(dve.tensor_tensor(sel2[:, 0], lg2[:, :, 4:12], hot4[:, :, 0:1].to_broadcast([P, NT, 8]), ALU.mult))
        for g in range(1, 4):
            step(dve.tensor_tensor(sel2[:, 1], lg2[:, :, 4 + 8 * g:12 + 8 * g],
                                   hot4[:, :, g:g + 1].to_broadcast([P, NT, 8]), ALU.mult))
            step(dve.tensor_tensor(sel2[:, 0], sel2[:, 0], sel2[:, 1], ALU.add))
        step(dve.tensor_reduce(top, sel2[:, 0], AX, ALU.max))
        first_hot(hot8[:, 0], sel2[:, 0], top, 8)
        step(dve.scalar_tensor_tensor(out=sel2[:, 1], in0=hot8[:, 0], scalar=-1e30, in1=sel2[:, 0], op0=ALU.mult,
                                      op1=ALU.add))
        step(dve.tensor_reduce(second, sel2[:, 1], AX, ALU.max))
        dve.tensor_tensor(r2[:, 5, :], second, top, ALU.subtract).then_inc(S["route2_b"], 1)
        first_hot(hot8[:, 1], sel2[:, 1], second, 8)
        for i in range(2):
            for g in range(4):
                steps.mark(dve.tensor_tensor(hot32[:, i, :, 8 * g:8 * g + 8], hot8[:, i],
                                             hot4[:, :, g:g + 1].to_broadcast([P, NT, 8]), ALU.mult))
        steps.wait()
        step(dve.tensor_tensor(hot32[:, 2], hot32[:, 0], hot32[:, 1], ALU.add))
        step(dve.memset(slotm[:, 0, 0, :], 0.0))
        for t in range(1, NT):
            step(dve.tensor_tensor(slotm[:, 0, t, :], slotm[:, 0, t - 1, :], hot32[:, 2, t - 1, :], ALU.add))
        dve.tensor_tensor(cnt[:, 5, :], slotm[:, 0, NT - 1, :], hot32[:, 2, NT - 1, :], ALU.add).then_inc(S["hot_ready"], 1)
        dve.wait_ge(S["route2_exp"], 2 + past["route2_exp"])
        step(dve.tensor_reduce(r2[:, 1, :], cand[:, :, 0:4], AX, ALU.add))
        step(dve.reciprocal(r2[:, 2, :], r2[:, 1, :]))
        step(dve.tensor_scalar(r2[:, 6, :], r2[:, 5, :], 1.0, None, ALU.add))
        step(dve.reciprocal(r2[:, 7, :], r2[:, 6, :]))
        step(dve.tensor_tensor(r2[:, 8, :], r2[:, 7, :], r2[:, 2, :], ALU.mult))
        step(dve.tensor_tensor(r2[:, 9, :], r2[:, 8, :], r2[:, 5, :], ALU.mult))
        dve.wait_ge(S["ranks"], 1 + past["ranks"])
        dve.wait_ge(S["route_consts"], 4 + past["route_consts"])
        step(dve.tensor_copy(cnt[:, 0, :], ps[:, 1, 0:E2]))
        step(dve.tensor_scalar(cnt[:, 1, :], cnt[:, 0, :], float(room), None, ALU.is_gt))
        for beyond in range(room + P, T, P):
            step(dve.scalar_tensor_tensor(out=cnt[:, 1, :], in0=cnt[:, 0, :], scalar=float(beyond), in1=cnt[:, 1, :],
                                          op0=ALU.is_gt, op1=ALU.add))
        step(dve.tensor_tensor_scan(cnt[:, 2, :], ones[:, 0:E2], cnt[:, 1, :], 0.0, ALU.mult, ALU.add))
        step(dve.tensor_tensor(cnt[:, 3, :], cnt[:, 2, :], cnt[:, 1, :], ALU.subtract))
        step(dve.tensor_scalar(cnt[:, 4, :], cnt[:, 3, :], float(P), float(E2 * P - room), ALU.mult, ALU.add))
        step(dve.tensor_tensor(cnt[:, 4, :], cnt[:, 4, :], cnt[:, 6, :], ALU.subtract))
        rank = ps[:, 0, 0:NT * E2].rearrange("p (t e) -> p t e", t=NT)
        where = slotm[:, 1]
        step(dve.tensor_scalar(where, rank, float(room), None, ALU.is_ge))
        step(dve.tensor_tensor(where, where, cnt[:, 4, :].unsqueeze(1).to_broadcast([P, NT, E2]), ALU.mult))
        step(dve.tensor_tensor(where, where, cnt[:, 6, :].unsqueeze(1).to_broadcast([P, NT, E2]), ALU.add))
        step(dve.tensor_tensor(where, where, rank, ALU.add))
        for i in range(2):
            step(dve.tensor_tensor(slotm[:, 0], where, hot32[:, i], ALU.mult))
            step(dve.tensor_reduce(r2[:, 10 + i, :], slotm[:, 0], AX, ALU.add))
            dve.tensor_copy(slot_u[:, i, :], r2[:, 10 + i, :]).then_inc(S["slots2"], 1)
        step(dve.tensor_tensor(oblk[:], cnt[:, 2, :].unsqueeze(1).to_broadcast([P, NOVF, E2]),
                               iota_b[:].unsqueeze(2).to_broadcast([P, NOVF, E2]), ALU.is_le))
        step(dve.tensor_reduce(oexp[:], oblk[:], AX, ALU.add))
        step(dve.tensor_scalar(oexp[:], oexp[:], float(E2 - 1), None, ALU.min))
        step(dve.tensor_copy(oexp_u[:, 0:NOVF], oexp[:]))
        dve.tensor_copy(oexp_u[:, NOVF:NOVF + 1], cnt[:, 2, E2 - 1:E2]).then_inc(S["ov_known"], 1)
        dve.wait_ge(S["tok_back"], 16 + past["tok_back"])
        dve.tensor_copy(tok_rows_f[:], tok_rows[:]).then_inc(S["tok_f"], 1)
        dve.wait_ge(S["tok_tr"], 1 + past["tok_tr"])
        step(dve.tensor_copy(tokc[:], ps[:, 2, 0:NBLK]))

        def tokens2(e, r):
            dve.tensor_copy(tok_in[r][:], tokc[:, bass.ds(e, 1)]).then_inc(S["m2_tok"], 1)

        def m2_lo(q, r, c):
            n, slot, wset, _ = m2_at(q, r, c)
            dve.wait_ge(S["m2_hi"], n + 1 + past["m2_hi"])
            dve.tensor_tensor(mL[:, wset, :], ring[:, slot, :], mH[:, wset, :].bitcast(F32),
                              ALU.subtract).then_inc(S["m2_lo"], 1)

        def x_lo2(e, r, j):
            dve.wait_ge(S["m2_xT_hi"], 2 * e + j + 1 + past["m2_xT_hi"])
            part = xsH[:, r, 4 * j:4 * j + 4, :].rearrange("p a b -> p (a b)")
            dve.tensor_tensor(xsL[:, r, 4 * j:4 * j + 4, :].rearrange("p a b -> p (a b)"), ps[:, 7 - j, :],
                              part.bitcast(F32), ALU.subtract).then_inc(S["m2_xT_lo"], 1)

        def hidden(e, r):
            dve.wait_ge(S["m2_silu"], e + 1 + past["m2_silu"])
            half = slice(512 * r, 512 * r + 512)
            dve.tensor_tensor(hid[:, half], sg[:, half], ps[:, 2 * r + 1, :], ALU.mult).then_inc(S["m2_hid"], 1)

        tokens2(0, 0)
        tokens2(1, 1)
        for j in range(2):
            x_lo2(0, 0, j)

        def m2_step(q, r):
            s = 2 * q + r
            if not (static(q) and s + 2 >= E2):
                dve.wait_ge(S["m2_xT"], 2 * s + 2 + past["m2_xT"])
                tokens2(s + 2, r)
            for c in range(12):
                if static(q) and s == 0 and c >= 8:
                    break
                if c == 1 and not (static(q) and s == 0):
                    hidden(s - 1, 1 - r)
                if c == 8 and not (static(q) and s == 0):
                    dve.wait_ge(S["m2_hT_hi"], s + past["m2_hT_hi"])
                    dve.tensor_tensor(hidL[:, 0:4, :].rearrange("p a b -> p (a b)"), ps[:, 6, :],
                                      hidH[:, 0:4, :].rearrange("p a b -> p (a b)").bitcast(F32),
                                      ALU.subtract).then_inc(S["m2_hT_lo"], 1)
                if c in (9, 11) and not (static(q) and s >= E2 - 1):
                    x_lo2(s + 1, 1 - r, (c - 9) // 2)
                if not (static(q) and s == E2 and c < 8):
                    m2_lo(q, r, c)
            if static(q) and s == 0:
                for j in range(2):
                    x_lo2(1, 1, j)

        m2_steps(dve, m2_step)

        def overflow(b):
            dve.wait_ge(S["ov_xT"], b + past["ov_xT"])
            dve.tensor_copy(otok[:], tokc[:, bass.ds(b + E2, 1)]).then_inc(S["ov_tok"], 1)
            dve.wait_ge(S["ov_silu"], b + 1 + past["ov_silu"])
            dve.tensor_tensor(hid[:, 0:512], sg[:, 0:512], ps[:, 1, :], ALU.mult).then_inc(S["ov_hid"], 1)

        overflow_blocks(dve, overflow)

        for t in range(NT):
            u = t % 2
            one_row, two_row, x_row = ring[:, u, :], ring[:, 2 + u, :], ring[:, 4 + u, :]
            dve.wait_ge(c_in[u], 48 * (t // 2 + 1))
            step(dve.tensor_scalar(one_row, one_row, r2[:, 8, t:t + 1], None, ALU.mult))
            step(dve.scalar_tensor_tensor(out=one_row, in0=two_row, scalar=r2[:, 9, t:t + 1], in1=one_row,
                                          op0=ALU.mult, op1=ALU.add))
            step(dve.tensor_tensor(one_row, one_row, gate_ffn_row[:], ALU.mult))
            dve.tensor_tensor(x_row, x_row, one_row, ALU.add).then_inc(S["x_final"], 1)
            dve.wait_ge(S["sq_final"], t + 1 + past["sq_final"])
            dve.tensor_scalar(stat[:, 9, 0:1], stat[:, 8, 0:1], 1.0 / D, EPS, ALU.mult, ALU.add).then_inc(S["var_final"], 1)
            dve.wait_ge(S["rstd_final"], t + 1 + past["rstd_final"])
            dve.wait_ge(S["final_in"], 16)
            if t >= 2:
                dve.wait_ge(c_out[u], 16 * (t // 2))
            dve.scalar_tensor_tensor(out=ring[:, 6 + u, :], in0=x_row, scalar=stat[:, 10, 0:1], in1=final_row[:],
                                     op0=ALU.mult, op1=ALU.mult).then_inc(S["final_done"], 1)

    @block.tensor
    def _(pe):
        def three(outs, high, low, rhs, start, stop):
            for o, (rh, rl) in zip(outs, rhs):
                pe.matmul(o, high, rh, start=start, stop=False)
                pe.matmul(o, high, rl, start=False, stop=False)
            for o, (rh, _) in zip(outs, rhs):
                last = pe.matmul(o, low, rh, start=False, stop=stop)
            return last

        def sum_columns(group):
            for c in range(KD):
                last = pe.matmul(ps[:, 7, bass.ds(256 + 8 * group + c, 1)], acc[:, c * P:(c + 1) * P], ones[:, 0:1],
                                 start=True, stop=True)
            last.then_inc(S["mod_mm"], 1)

        pe.wait_ge(S["consts"], 4)
        pe.wait_ge(S["rows_in"], 16 * (len(row_at[0]) + len(row_at[1])))
        for b in range(2):
            pe.transpose(ps[:, 7, b * P:(b + 1) * P], rows[:, b, :], ident[:]).then_inc(S["cols_tr"], 1)
        for j in range(2):
            pe.wait_ge(S["ada_done"], KD * (j + 1))
            sum_columns(j)
        for g in range(16):
            half, c = g // KD, g % KD
            pe.wait_ge(S["xn_done"], 4 * half + 4)
            if g >= 4:
                pe.wait_ge(S["tr_lo"], g - 3)
            for j in range(4):
                last = pe.transpose(ps[:, g % 4, j * P:(j + 1) * P], xz[:, 4 * half + j, c * P:(c + 1) * P], ident[:])
            last.then_inc(S["tr_ready"], 1)

        def f_step(q, r):
            f = 2 * q + r
            for p in range(3):
                pe.wait_ge(S["split_done"], 3 * f + p + 1)
                if static(q) and f == 0:
                    pe.wait_ge(S["tr_lo"], 16)
                else:
                    pe.wait_ge(S[("c_copied", "cv_done", "z_done")[p]], f)
                for k in range(KD):
                    last = three([ps[:, 2 * p + h, :] for h in range(2)],
                                 wH[:, p, k * P:(k + 1) * P], wL[:, p, k * P:(k + 1) * P],
                                 [(hH[:, k, 512 * h:512 * h + 512], hL[:, k, 512 * h:512 * h + 512]) for h in range(2)],
                                 k == 0, k == KD - 1)
                last.then_inc(S["f_part"], 1)
                if p == 0 and r == 0 and not (static(q) and q == 0):
                    pe.wait_ge(S["ada_done"], 8 * q + 16)
                    sum_columns(q + 1)

        in_pairs(pe, KD, f_step)
        pe.wait_ge(S["ada_done"], 6 * KD)
        sum_columns(5)

        def output_stage(b, rows_n, router, width):
            for n in range(rows_n):
                if n >= 2:
                    pe.wait_ge(S["bc_done" + b], n - 1 + past["bc_done" + b])
                for c in range(KD):
                    pe.wait_ge(S["diag_ready" + b], 8 * n + c + 1 + past["diag_ready" + b])
                    pe.matmul(ps[:, 2 * (n % 2) + c // 4, (c % 4) * P:(c % 4 + 1) * P], ones[:], diag[:, c % 2, :],
                              start=True, stop=True).then_inc(S["diag_used" + b], 1)
            pe.wait_ge(S["bc_done" + b], rows_n + past["bc_done" + b])

            def o_step(q, r):
                s = 2 * q + r
                if not (static(q) and s == NT):
                    pe.wait_ge(S["zs_lo" + b], s + 1 + past["zs_lo" + b])
                    if not (static(q) and s < 2):
                        pe.wait_ge(S["x1_done" + b], s - 1 + past["x1_done" + b])
                    for k in range(KD):
                        last = three([ps[:, 2 * r + n, :] for n in range(2)], zsH[:, r, k, :], zsL[:, r, k, :],
                                     [(woH[:, k, 512 * n:512 * n + 512], woL[:, k, 512 * n:512 * n + 512])
                                      for n in range(2)], k == 0, k == KD - 1)
                    last.then_inc(S["y_ready" + b], 1)
                if b == "" and (not static(q) or 1 <= s <= 6):
                    pe.wait_ge(S["ada_done"], 8 * s + 48)
                    sum_columns(s + 5)
                if static(q) and s == 0:
                    return
                pe.wait_ge(S["h2_done" + b], s + past["h2_done" + b])
                for c in range(KD):
                    last = pe.transpose(ps[:, 4 + c // 4, (c % 4) * P:(c % 4 + 1) * P], h2t[:, c * P:(c + 1) * P],
                                        ident[:])
                last.then_inc(S["tr2" + b], 1)
                pe.wait_ge(S["h2T_ready" + b], s + past["h2T_ready" + b])
                for k in range(KD):
                    last = pe.matmul(ps[:, 6, bass.ds((s - 1) * width, width)], h2T[:, k, :], router[:, k, :],
                                     start=(k == 0), stop=(k == KD - 1))
                last.then_inc(S["rt_done" + b], 1)

            in_pairs(pe, NT + 1, o_step)

        pe.wait_ge(S["small_in"], 16 * 8)
        output_stage("", 4, router1, E1)

        pe.wait_ge(S["aff_ready"], 1)
        for t in range(NT):
            last = pe.transpose(ps[0:E1, t // 4, (t % 4) * P:(t % 4 + 1) * P], aff[:, t, :], ident[:])
        last.then_inc(S["affT_tr"], 1)
        pe.wait_ge(S["top_ready"], 1 + past["top_ready"])
        pe.transpose(ps[:, 2, 0:E1], top_v[:], ident[0:E1, 0:E1])
        pe.transpose(ps[:, 2, E1:2 * E1], top_f[:], ident[0:E1, 0:E1]).then_inc(S["topT_tr"], 1)

        def x_transposes(e, r, lot):
            pe.wait_ge(xs_in[r], lot)
            for j in range(2):
                if not (static(e) and e == 0):
                    pe.wait_ge(S["m1_xT_lo"], 2 * e + j - 1)
                for c in range(4):
                    last = pe.transpose(ps[:, 6 + j, c * P:(c + 1) * P], xs[r][:, (4 * j + c) * P:(4 * j + c + 1) * P],
                                        ident[:])
                last.then_inc(S["m1_xT"], 1)

        pe.wait_ge(S["slots_ready"], 1)
        x_transposes(0, 0, 16)

        def h_transposes(e, j):
            pe.wait_ge(S["m1_hid"], 2 * e + j + 1)
            for c in range(4):
                last = pe.transpose(ps[:, 2 * j, c * P:(c + 1) * P], hid[:, (4 * j + c) * P:(4 * j + c + 1) * P],
                                    ident[:])
            last.then_inc(S["m1_hT"], 1)

        def m1_step(q, r):
            e = 2 * q + r
            first = static(q) and e == 0
            pe.wait_ge(S["m1_xT_lo"], 2 * e + 2)
            for m in range(24):
                pe.wait_ge(S["m1_lo"], 24 * e + m + 1)
                if m < 16:
                    n, kp, u = m // 8, (m % 8) // 2, m % 2
                    bank = ps[:, n + 2 * u, :]
                    if m % 8 == 0 and not first:
                        pe.wait_ge(S["m1_hid"], 2 * e + n - 1)
                        pe.wait_ge(S["m1_hT_lo"], 2 * e)
                    for k2 in range(2):
                        k = 2 * kp + k2
                        w = slice(512 * k2, 512 * k2 + 512)
                        last = three([bank], xsH[:, r, k, :], xsL[:, r, k, :],
                                     [(mH[:, m % WSETS, w], mL[:, m % WSETS, w])], k == 0, k == KD - 1)
                else:
                    k = m - 16
                    if k == 0 and not first:
                        pe.wait_ge(S["m1_y_done"], e)
                    if k % 4 == 0:
                        pe.wait_ge(S["m1_hT_lo"], 2 * e + k // 4 + 1)
                    last = three([ps[:, 4 + n, :] for n in range(2)], hidH[:, k, :], hidL[:, k, :],
                                 [(mH[:, m % WSETS, 512 * n:512 * n + 512], mL[:, m % WSETS, 512 * n:512 * n + 512])
                                  for n in range(2)], k == 0, k == KD - 1)
                last.then_inc(S["m1_used"], 1)
                if m == 13:
                    h_transposes(e, 0)
                if m == 15:
                    if not (static(q) and e == E1 - 1):
                        x_transposes(e + 1, 1 - r, 16 * q + (16 if r == 0 else 32))
                    h_transposes(e, 1)

        in_pairs(pe, E1, m1_step)

        for g in range(16):
            half, c = g // KD, g % KD
            pe.wait_ge(S["xn_done_2"], 4 * half + 4 + past["xn_done_2"])
            if g >= 4:
                pe.wait_ge(S["tr_lo_2"], g - 3 + past["tr_lo_2"])
            for j in range(4):
                last = pe.transpose(ps[:, g % 4, j * P:(j + 1) * P], xz[:, 4 * half + j, c * P:(c + 1) * P], ident[:])
            last.then_inc(S["tr_ready_2"], 1)
        pe.wait_ge(S["tr_lo_2"], 16 + past["tr_lo_2"])
        for m in range(4):
            pe.wait_ge(S["d2_split"], m + 1 + past["d2_split"])
            for k2 in range(2):
                k, w = 2 * m + k2, slice(512 * k2, 512 * k2 + 512)
                for t in range(NT):
                    last = three([ps[:, t, :]], gH[:, k, t * P:(t + 1) * P], gL[:, k, t * P:(t + 1) * P],
                                 [(uH[:, m % 2, w], uL[:, m % 2, w])], k == 0, k == KD - 1)
            last.then_inc(S["d2_part"], 1)
        pe.wait_ge(S["v_odd"], 4)
        pe.wait_ge(S["if_lo"], 1)
        for t in range(NT):
            for k in range(KD):
                last = three([ps[:, 7, 8 * t:8 * t + 8]], gH[:, k, t * P:(t + 1) * P], gL[:, k, t * P:(t + 1) * P],
                             [(w_ifH[:, k, :], w_ifL[:, k, :])], k == 0, k == KD - 1)
        last.then_inc(S["if_mm"], 1)
        pe.wait_ge(S["gt_ready"], 1)
        pe.wait_ge(S["v_even"], 4)
        for t in range(NT):
            pe.transpose(ps[0:4, 4 + t // 4, (t % 4) * P:(t % 4 + 1) * P], gt[:, t, 0:4], ident[:])
            last = pe.transpose(ps[0:4, 6 + t // 4, (t % 4) * P:(t % 4 + 1) * P], gt[:, t, 4:8], ident[:])
        last.then_inc(S["gt_tr"], 1)

        for i in range(12):
            m, bank = 4 + i, 2 * (i % 4)
            if i == 2:
                pe.wait_ge(S["gate_in"], 1 + past["gate_in"])
            if i == 3:
                pe.wait_ge(S["gate_rows"], 1 + past["gate_rows"])
            if i == 4:
                pe.wait_ge(S["d2_out"], 1)
                pe.wait_ge(S["gate_m"], 1 + past["gate_m"])
                pe.wait_ge(S["floor"], 1 + past["floor"])
                for j, row in enumerate((4, 6)):
                    for t in range(NT):
                        last = pe.transpose(ps[:, 0, 32 * j + 4 * t:32 * j + 4 * t + 4],
                                            xz[0:4, row, t * P:(t + 1) * P], ident[0:4, 0:4])
                last.then_inc(S["gate_cols"], 1)
                pe.wait_ge(S["gcol_ready"], 2 + past["gcol_ready"])
            if i >= 4:
                pe.wait_ge(S["d2_out"], i - 3)
            pe.wait_ge(S["d2_split"], m + 1 + past["d2_split"])
            for k in range(KD):
                last = three([ps[:, bank + h, :] for h in range(2)],
                             uH[:, m % 2, k * P:(k + 1) * P], uL[:, m % 2, k * P:(k + 1) * P],
                             [(gH[:, k, 512 * h:512 * h + 512], gL[:, k, 512 * h:512 * h + 512]) for h in range(2)],
                             k == 0, k == KD - 1)
            last.then_inc(S["d2_part"], 1)

        def pair_matmul(bank, lhsT, rhs, n=T):
            for at in range(0, n, 512):
                size = min(512, n - at)
                last = pe.matmul(ps[:, bank + at // 512, 0:size], lhsT, rhs[:, at:at + size], start=True, stop=True)
            return last

        pe.wait_ge(S["cell_in"], 48)
        pe.wait_ge(S["d2_out"], 12)
        pe.wait_ge(S["branch"], 8)
        for g in range(4):
            if g >= 2:
                pe.wait_ge(S["pool_out"], g - 1)
            pair_matmul(2 * (g % 2), wp[:, g, :], xz[:, 4 + g, :]).then_inc(S["pool_mm"], 1)

        offs = [P * sum(NT - j for j in range(s)) for s in range(NT)]

        def head_scores(h):
            if h >= 2:
                pe.wait_ge(S["hy_done"], h - 1)
                pe.wait_ge(S["num_out"], NT * (h - 1))
            pe.wait_ge(S["uc_ready"], h + 1)
            if h == 1:
                pe.wait_ge(S["m_out"], 1)
            pair_matmul(4, wq[:, h, :], xz[:, h, :]).then_inc(S["q_mm"], 1)
            if h == 1:
                pe.wait_ge(S["k_out"], 1)
            pair_matmul(6, wk[:, h, :], xz[:, h, :]).then_inc(S["k_mm"], 1)
            pe.wait_ge(S["pick"], 2 + past["pick"])
            pe.wait_ge(S["neg_ready"], 1 + past["neg_ready"])
            pe.wait_ge(S["q_out"], h + 1)
            pair_matmul(4, pick[:, h, :], negM[:]).then_inc(S["m_mm"], 1)
            pe.wait_ge(S["k_out"], h + 1)
            for s in range(NT):
                i = NT * h + s
                if i >= 2:
                    pe.wait_ge(S["pm_ready"], i - 1)
                else:
                    pe.wait_ge(S["pool_out"], 3 + i)
                pair_matmul(2 * (i % 2), kT[:, h % 2, P * s:P * s + P], qT[:, h % 2, P * s:T],
                            T - P * s).then_inc(S["s_mm"], 1)

        def head_values(h):
            pe.wait_ge(S["pm_ready"], NT * h + NT)
            pe.wait_ge(S["k_out"], min(h + 2, 4))
            pe.wait_ge(S["ones_col"], 1 + past["ones_col"])
            for t in range(NT):
                i = NT * h + t
                if i >= 2:
                    pe.wait_ge(S["num_out"], i - 1)
                for s in range(t + 1):
                    last = pe.matmul(ps[:, 6 + t % 2, 0:P + 1], pm[:, h % 2, offs[s] + P * (t - s):offs[s] + P * (t - s + 1)],
                                     vt[:, s, h, :], start=(s == 0), stop=(s == t))
                last.then_inc(S["pv"], 1)
            pe.wait_ge(S["hn_ready"], h + 1)
            pe.wait_ge(S["m_out"], min(h + 2, 4))
            for t in range(NT):
                last = pe.transpose(ps[:, 4 + t // 4, (t % 4) * P:(t % 4 + 1) * P], num[:, t, 0:P], ident[:])
            last.then_inc(S["hn_tr"], 1)

        head_scores(0)
        for h in range(4):
            if h < 3:
                head_scores(h + 1)
            head_values(h)
        pe.wait_ge(S["small_in"], 16 * 8)
        output_stage("_2", 4, router2, NR2)

        pe.wait_ge(S["masks"], 5)
        pe.wait_ge(S["hot_ready"], 1 + past["hot_ready"])
        pe.matmul(ps[:, 0, 0:NT * E2], ones[:], slotm[:, 0].rearrange("p t e -> p (t e)"), start=True, stop=False)
        pe.matmul(ps[:, 0, 0:NT * E2], tri[:], hot32[:, 2].rearrange("p t e -> p (t e)"), start=False, stop=True)
        pe.matmul(ps[:, 1, 0:E2], ones[:], cnt[:, 5, :], start=True, stop=True).then_inc(S["ranks"], 1)
        pe.wait_ge(S["tok_f"], 1 + past["tok_f"])
        pe.transpose(ps[:, 2, 0:NBLK], tok_rows_f[:], ident[0:NBLK, 0:NBLK]).then_inc(S["tok_tr"], 1)

        def x_transposes2(e, r, j, lot):
            pe.wait_ge(xs_in[r], lot + XS_PAST)
            for c in range(4):
                last = pe.transpose(ps[:, 7 - j, c * P:(c + 1) * P], xs[r][:, (4 * j + c) * P:(4 * j + c + 1) * P],
                                    ident[:])
            last.then_inc(S["m2_xT"], 1)

        pe.wait_ge(S["m2_tok"], 1 + past["m2_tok"])
        for j in range(2):
            x_transposes2(0, 0, j, 16)

        def m2_step(q, r):
            s = 2 * q + r
            first, final = static(q) and s == 0, static(q) and s == E2
            if not final:
                pe.wait_ge(S["m2_xT_lo"], 2 * s + 2 + past["m2_xT_lo"])
                if not (static(q) and s < 2):
                    pe.wait_ge(S["m2_hid"], s - 1 + past["m2_hid"])
            for c in range(12):
                n, _, wset, _ = m2_at(q, r, c)
                if first and c >= 8:
                    break
                if c < 8 and not final:
                    pe.wait_ge(S["m2_lo"], n + 1 + past["m2_lo"])
                    for k2 in range(2):
                        k, w = 2 * (c // 2) + k2, slice(512 * k2, 512 * k2 + 512)
                        last = three([ps[:, 2 * r + c % 2, :]], xsH[:, r, k, :], xsL[:, r, k, :],
                                     [(mH[:, wset, w], mL[:, wset, w])], k == 0, k == KD - 1)
                    last.then_inc(S["m2_used"], 1)
                if c == 1 and not first:
                    pe.wait_ge(S["m2_hid"], s + past["m2_hid"])
                    for j in range(4):
                        at = 512 * (1 - r) + j * P
                        last = pe.transpose(ps[:, 6, j * P:(j + 1) * P], hid[:, at:at + P], ident[:])
                    last.then_inc(S["m2_hT"], 1)
                if c in (3, 5) and not (static(q) and s >= E2 - 1):
                    j = (c - 3) // 2
                    if j == 1 and not first:
                        pe.wait_ge(S["m2_hT_lo"], s + past["m2_hT_lo"])
                    x_transposes2(s + 1, 1 - r, j, 16 * q + (16 if r == 0 else 32))
                if c >= 8:
                    if c == 8:
                        pe.wait_ge(S["m2_hT_lo"], s + past["m2_hT_lo"])
                        if not (static(q) and s < 2):
                            pe.wait_ge(S["m2_y"], s - 1)
                    pe.wait_ge(S["m2_lo"], n + 1 + past["m2_lo"])
                    k = c - 8
                    last = three([ps[:, 4 + h, :] for h in range(2)], hidH[:, k, :], hidL[:, k, :],
                                 [(mH[:, wset, 512 * h:512 * h + 512], mL[:, wset, 512 * h:512 * h + 512])
                                  for h in range(2)], k == 0, k == 3)
                    last.then_inc(S["m2_used"], 1)

        m2_steps(pe, m2_step)

        def overflow_landed(b, c):
            pe.wait_ge(ring_in[c], 16 * (used2[c] + E2 + 1) + 16 * b)

        def overflow(b):
            pe.wait_ge(xs_in[0], 16 * b + 16 + XS_PAST + 16 * (E2 // 2))
            for c in range(KD):
                last = pe.transpose(ps[:, 6 + c // 4, (c % 4) * P:(c % 4 + 1) * P], xs[0][:, c * P:(c + 1) * P], ident[:])
            last.then_inc(S["ov_xT"], 1)
            pe.wait_ge(S["ov_x"], b + 1 + past["ov_x"])
            for c in range(8):
                overflow_landed(b, c)
                for k2 in range(2):
                    k = 2 * (c // 2) + k2
                    last = pe.matmul(ps[:, c % 2, :], oxT[:, k, :], ring[:, c, 512 * k2:512 * k2 + 512],
                                     start=(k == 0), stop=(k == KD - 1))
            last.then_inc(S["ov_gu"], 1)
            pe.wait_ge(S["ov_hid"], b + 1 + past["ov_hid"])
            for j in range(4):
                last = pe.transpose(ps[:, 6, j * P:(j + 1) * P], hid[:, j * P:(j + 1) * P], ident[:])
            last.then_inc(S["ov_hT"], 1)
            pe.wait_ge(S["ov_h"], b + 1 + past["ov_h"])
            for k in range(4):
                overflow_landed(b, 8 + k)
                for h in range(2):
                    last = pe.matmul(ps[:, 4 + h, :], ohT[:, k, :], ring[:, 8 + k, 512 * h:512 * h + 512],
                                     start=(k == 0), stop=(k == 3))
            last.then_inc(S["ov_down"], 1)

        overflow_blocks(pe, overflow)


SHAPES = {
    "x": (T, D), "c": (8, P), "c_2": (8, P), "ada_w": (D, 6 * D), "ada_b": (48, P), "norm_g": (16, P),
    "sc_w_in": (D, 3 * D), "sc_conv": (24, P), "sc_w_out": (D, D), "moe_router": (D, E1),
    "moe_w_gate": (E1, D, D), "moe_w_up": (E1, D, D), "moe_w_down": (E1, D, D),
    "ada_w_2": (D, 6 * D), "ada_b_2": (48, P), "norm1_g_2": (8, P), "norm2_g_2": (8, P),
    "w_in_2": (D, 2056), "conv_w_2": (16, P), "conv_b_2": (4, P), "w_q_2": (4, P, P), "w_k_2": (4, P, P),
    "b_igate_2": (4, 1), "b_fgate_2": (4, 1), "mlstm_norm_g_2": (4, P), "mlstm_skip_2": (4, P),
    "w_pool_2": (4, P, P), "b_pool_2": (4, P), "pool_scale_2": (4, P), "w_out_2": (D, D),
    "w_router_group_2": (D, 4), "b_router_group_2": (1, 4), "w_router_expert_2": (D, E2),
    "b_router_expert_2": (1, E2), "w_expert_gate_2": (E2, D, F2), "w_expert_up_2": (E2, D, F2),
    "w_expert_down_2": (E2, F2, D), "final_g_2": (8, P),
}


def kernel(**inputs):
    import numpy as np
    import concourse.bacc as bacc
    from concourse.bass_utils import run_bass_kernel_spmd

    nc = bacc.Bacc("TRN2", target_bir_lowering=False, num_devices=1)
    arrays, io = {}, {}
    for name, shape in SHAPES.items():
        arrays[f"in_{name}"] = np.ascontiguousarray(inputs[name]).reshape(shape)
        io[name] = nc.dram_tensor(f"in_{name}", shape, F32, kind="ExternalInput").ap()
    out = nc.dram_tensor("out", (T, D), F32, kind="ExternalOutput").ap()
    program(nc, io, out)
    done = run_bass_kernel_spmd(nc, [arrays], core_ids=[0])
    return done.results[0]["out"].reshape(1, T, D)
```
